# Optimizing a Trainium2 kernel written in Bass

```python
import math
import jax, jax.numpy as jnp
from jax import lax
import numpy as np

D_MODEL = 1024
BATCH = 1
SEQ = 512
DEPTH = 1

D_MIX = D_MODEL
MLSTM_WIDTH = D_MIX // 2
N_MLSTM_HEADS = 4
HEAD_DIM = MLSTM_WIDTH // N_MLSTM_HEADS
POOL_WIDTH = D_MIX - MLSTM_WIDTH
POOL_WINDOWS = (2, 4, 8, 16)
N_POOL_GROUPS = len(POOL_WINDOWS)
POOL_GROUP_DIM = POOL_WIDTH // N_POOL_GROUPS
CONV_WIDTH = 4
CHUNK = 64
D_FF = 2816
EPS = 1e-6
OFF_QK = 0
OFF_V = 2 * MLSTM_WIDTH
OFF_O = 3 * MLSTM_WIDTH
OFF_G = 4 * MLSTM_WIDTH
OFF_P = OFF_G + 2 * N_MLSTM_HEADS
D_IN_PROJ = OFF_P + POOL_WIDTH

kernel_name = "hymba_mlstm_pool_macaron"

def rmsnorm(x, g):
    xf = x.astype(jnp.float32)
    y = xf * lax.rsqrt(jnp.mean(xf * xf, axis=-1, keepdims=True) + EPS)
    return (y * g.astype(jnp.float32)).astype(x.dtype)

def swiglu(h, w_gate, w_up, w_down):
    return (jax.nn.silu(h @ w_gate) * (h @ w_up)) @ w_down

def causal_dwconv(u, w, b):
    k_w, c = w.shape
    y = lax.conv_general_dilated(
        u, w[:, None, :].astype(u.dtype), window_strides=(1,),
        padding=[(k_w - 1, 0)], dimension_numbers=('NWC', 'WIO', 'NWC'),
        feature_group_count=c)
    return y + b.astype(u.dtype)

def mlstm_chunkwise(q, k, v, i_pre, f_pre):
    bsz, s, nh, d = q.shape
    nc = s // CHUNK
    to_chunks = lambda t: t.reshape(bsz, nc, CHUNK, nh, d).transpose(0, 3, 1, 2, 4)
    gate_chunks = lambda t: t.reshape(bsz, nc, CHUNK, nh).transpose(0, 3, 1, 2)
    qc = to_chunks(q)
    kc = to_chunks(k) * (d ** -0.5)
    vc = to_chunks(v)
    ig = gate_chunks(i_pre)
    bcum = jnp.cumsum(jax.nn.log_sigmoid(gate_chunks(f_pre)), axis=-1)

    def step(carry, inp):
        c_st, n_st, m_st = carry
        k_c, v_c, b_c, i_c = inp
        g = b_c[..., -1]
        a = g[..., None] - b_c + i_c
        m_new = jnp.maximum(g + m_st, jnp.max(a, axis=-1))
        w = jnp.exp(a - m_new[..., None])
        decay = jnp.exp(g + m_st - m_new)
        c_new = decay[..., None, None] * c_st + jnp.einsum('bhlk,bhlv->bhkv', k_c * w[..., None], v_c)
        n_new = decay[..., None] * n_st + jnp.einsum('bhl,bhlk->bhk', w, k_c)
        return (c_new, n_new, m_new), (c_st, n_st, m_st)

    init = (jnp.zeros((bsz, nh, d, d), jnp.float32),
            jnp.zeros((bsz, nh, d), jnp.float32),
            jnp.zeros((bsz, nh), jnp.float32))
    xs = (jnp.moveaxis(kc, 2, 0), jnp.moveaxis(vc, 2, 0),
          jnp.moveaxis(bcum, 2, 0), jnp.moveaxis(ig, 2, 0))
    _, (c_prev, n_prev, m_prev) = lax.scan(step, init, xs)
    c_prev = jnp.moveaxis(c_prev, 0, 2)
    n_prev = jnp.moveaxis(n_prev, 0, 2)
    m_prev = jnp.moveaxis(m_prev, 0, 2)

    causal = jnp.tril(jnp.ones((CHUNK, CHUNK), dtype=bool))
    inter_log = bcum + m_prev[..., None]
    dlog = bcum[..., :, None] - bcum[..., None, :] + ig[..., None, :]
    dlog = jnp.where(causal, dlog, -jnp.inf)
    m_t = jnp.maximum(inter_log, jnp.max(dlog, axis=-1))
    dw = jnp.exp(dlog - m_t[..., None])
    inter_w = jnp.exp(inter_log - m_t)
    scores = jnp.einsum('bhcld,bhcsd->bhcls', qc, kc) * dw
    num = (jnp.einsum('bhcls,bhcsd->bhcld', scores, vc)
           + inter_w[..., None] * jnp.einsum('bhcld,bhcdv->bhclv', qc, c_prev))
    qn = jnp.sum(scores, axis=-1) + inter_w * jnp.einsum('bhcld,bhcd->bhcl', qc, n_prev)
    den = jnp.maximum(jnp.abs(qn), jnp.exp(-m_t))
    h = num / den[..., None]
    return h.transpose(0, 2, 3, 1, 4).reshape(bsz, s, nh * d)

def multiscale_pool(u, pool_w, pool_scale):
    bsz, s, _ = u.shape
    pos = jnp.arange(1, s + 1, dtype=jnp.int32)
    outs = []
    for gi, win in enumerate(POOL_WINDOWS):
        ug = u[..., gi * POOL_GROUP_DIM:(gi + 1) * POOL_GROUP_DIM].astype(jnp.float32)
        cs = jnp.cumsum(ug, axis=1)
        lag = jnp.pad(cs, ((0, 0), (win, 0), (0, 0)))[:, :s]
        count = jnp.minimum(pos, win).astype(jnp.float32)
        outs.append((cs - lag) / count[None, :, None] - ug)
    pooled = jnp.stack(outs, axis=2)
    mixed = jnp.einsum('bsgc,gcd->bsgd', pooled, pool_w.astype(jnp.float32))
    return mixed.reshape(bsz, s, POOL_WIDTH) * pool_scale.astype(jnp.float32)

def setup_inputs(seed: int = 0) -> dict:
    key = jax.random.key(seed)
    ks = jax.random.split(key, 24)
    nrm = lambda k, shape, scale: jax.random.normal(k, shape, jnp.float32) * scale
    gain = lambda k, shape: 1.0 + 0.1 * jax.random.normal(k, shape, jnp.float32)
    col_scale = jnp.ones((D_IN_PROJ,), jnp.float32).at[OFF_G:OFF_P].set(0.1)
    w_in = nrm(ks[5], (DEPTH, D_MODEL, D_IN_PROJ), D_MODEL ** -0.5) * col_scale
    b_i = nrm(ks[6], (DEPTH, N_MLSTM_HEADS), 0.1)
    b_f = jnp.linspace(3.0, 6.0, N_MLSTM_HEADS, dtype=jnp.float32)[None, :] + nrm(ks[7], (DEPTH, N_MLSTM_HEADS), 0.1)
    return {
        "x": nrm(ks[0], (BATCH, SEQ, D_MODEL), 1.0),
        "ffn1_norm": gain(ks[1], (DEPTH, D_MODEL)),
        "ffn1_w_gate": nrm(ks[2], (DEPTH, D_MODEL, D_FF), D_MODEL ** -0.5),
        "ffn1_w_up": nrm(ks[3], (DEPTH, D_MODEL, D_FF), D_MODEL ** -0.5),
        "ffn1_w_down": nrm(ks[4], (DEPTH, D_FF, D_MODEL), D_FF ** -0.5),
        "mix_norm": gain(ks[8], (DEPTH, D_MODEL)),
        "w_in": w_in,
        "b_gates": jnp.concatenate([b_i, b_f], axis=-1),
        "conv_w": nrm(ks[9], (DEPTH, CONV_WIDTH, 2 * MLSTM_WIDTH), CONV_WIDTH ** -0.5),
        "conv_b": nrm(ks[10], (DEPTH, 2 * MLSTM_WIDTH), 0.01),
        "mh_norm": gain(ks[11], (DEPTH, MLSTM_WIDTH)),
        "pool_w": nrm(ks[12], (DEPTH, N_POOL_GROUPS, POOL_GROUP_DIM, POOL_GROUP_DIM), POOL_GROUP_DIM ** -0.5),
        "pool_scale": gain(ks[13], (DEPTH, POOL_WIDTH)),
        "w_out": nrm(ks[14], (DEPTH, D_MIX, D_MODEL), D_MIX ** -0.5),
        "ffn2_norm": gain(ks[15], (DEPTH, D_MODEL)),
        "ffn2_w_gate": nrm(ks[16], (DEPTH, D_MODEL, D_FF), D_MODEL ** -0.5),
        "ffn2_w_up": nrm(ks[17], (DEPTH, D_MODEL, D_FF), D_MODEL ** -0.5),
        "ffn2_w_down": nrm(ks[18], (DEPTH, D_FF, D_MODEL), D_FF ** -0.5),
        "final_norm": gain(ks[19], (D_MODEL,)),
    }

def reference(x, ffn1_norm, ffn1_w_gate, ffn1_w_up, ffn1_w_down, mix_norm, w_in, b_gates,
              conv_w, conv_b, mh_norm, pool_w, pool_scale, w_out, ffn2_norm, ffn2_w_gate,
              ffn2_w_up, ffn2_w_down, final_norm):
    bsz, s, _ = x.shape
    for l in range(DEPTH):
        x = x + 0.5 * swiglu(rmsnorm(x, ffn1_norm[l]), ffn1_w_gate[l], ffn1_w_up[l], ffn1_w_down[l])

        h = rmsnorm(x, mix_norm[l])
        proj = h @ w_in[l]
        qk = jax.nn.silu(causal_dwconv(proj[..., OFF_QK:OFF_V], conv_w[l], conv_b[l]))
        q = qk[..., :MLSTM_WIDTH].astype(jnp.float32).reshape(bsz, s, N_MLSTM_HEADS, HEAD_DIM)
        k = qk[..., MLSTM_WIDTH:].astype(jnp.float32).reshape(bsz, s, N_MLSTM_HEADS, HEAD_DIM)
        v = proj[..., OFF_V:OFF_O].astype(jnp.float32).reshape(bsz, s, N_MLSTM_HEADS, HEAD_DIM)
        o_gate = jax.nn.sigmoid(proj[..., OFF_O:OFF_G].astype(jnp.float32))
        gates = proj[..., OFF_G:OFF_P].astype(jnp.float32) + b_gates[l].astype(jnp.float32)
        i_pre = gates[..., :N_MLSTM_HEADS]
        f_pre = gates[..., N_MLSTM_HEADS:]

        hm = mlstm_chunkwise(q, k, v, i_pre, f_pre).reshape(bsz, s, N_MLSTM_HEADS, HEAD_DIM)
        hm = hm * lax.rsqrt(jnp.mean(hm * hm, axis=-1, keepdims=True) + EPS)
        hm = o_gate * (hm.reshape(bsz, s, MLSTM_WIDTH) * mh_norm[l].astype(jnp.float32))

        hp = multiscale_pool(proj[..., OFF_P:], pool_w[l], pool_scale[l])

        mix = jnp.concatenate([hm, hp], axis=-1).astype(x.dtype) @ w_out[l]
        x = x + mix

        x = x + 0.5 * swiglu(rmsnorm(x, ffn2_norm[l]), ffn2_w_gate[l], ffn2_w_up[l], ffn2_w_down[l])
    return rmsnorm(x, final_norm)


_drawn_inputs = setup_inputs


def setup_inputs(seed=0):
    import zlib

    import numpy as np

    out = dict(_drawn_inputs(seed))
    spreads = {}
    factors = {'conv_b': 24.57}
    for name, (base, spread) in spreads.items():
        noise = np.random.default_rng([zlib.crc32(name.encode()), seed]).standard_normal(out[name].shape)
        drawn = base * np.exp(spread * noise) if base else spread * noise
        out[name] = __import__('jax').numpy.asarray(drawn.astype(out[name].dtype))
    for name, factor in factors.items():
        out[name] = (out[name] * factor).astype(out[name].dtype)
    return out
```

```python
from contextlib import ExitStack

import numpy as np

import concourse.bass as bass
from concourse import mybir

F32 = mybir.dt.float32
F32R = mybir.dt.float32r
I32 = mybir.dt.int32
ALU = mybir.AluOpType
ACT = mybir.ActivationFunctionType

P = 128
T = 512
D = 1024
KD = D // P
FF = 2816
FB = FF // P
HEADS = 4
TB = T // P
EPS = 1e-6
K_SCALE = float(P) ** -0.5
WINDOWS = (2, 4, 8, 16)
MAXWIN = 16
TINY = 1e-37
RSQRT_SEED = float(0x5F3759DF)

UNIT = 8 * P
SLOTS = 4
RAWS = 2
DN_UNITS = 3
UP1 = 0
DN1 = UP1 + 2 * FB
MIX = DN1 + DN_UNITS * KD
QK_UNIT = MIX + 1
V_UNIT = QK_UNIT + 2 * HEADS
O_UNIT = V_UNIT + 4
PL_UNIT = O_UNIT + HEADS
WO_UNIT = PL_UNIT + HEADS
UP2 = WO_UNIT + KD
DN2 = UP2 + 2 * FB
N_UNITS = DN2 + DN_UNITS * KD

V_GAIN = 0
V_CONVW = V_GAIN + 4 * KD
V_CONVB = V_CONVW + 4 * KD
V_MH = V_CONVB + KD
V_PSC = V_MH + HEADS
V_BG = V_PSC + HEADS
V_MEAN_D = V_BG + 1
V_MEAN_H = V_MEAN_D + 1
V_INV = V_MEAN_H + 1
N_VEC = V_INV + HEADS * MAXWIN

S_OFF = {0: 0, 1: 512, 3: 896, 2: 1024}
S_COLS = 1280


def build_layer(nc, weights, pool_w, x_t, vecs, consts, out):
    ctx = ExitStack()
    with ctx:
        def sb(name, shape, dt=F32):
            return ctx.enter_context(nc.sbuf_tensor(name, shape, dt))

        def sem(name):
            return ctx.enter_context(nc.semaphore(name))

        raw = sb("raw", [P, RAWS, UNIT])
        w_hi = sb("w_hi", [P, SLOTS, UNIT], F32R)
        w_lo = sb("w_lo", [P, SLOTS, UNIT], F32R)
        x = sb("x", [P, KD, T])
        xg_hi = sb("xg_hi", [P, KD, T], F32R)
        xg_lo = sb("xg_lo", [P, KD, T], F32R)
        act_hi = sb("act_hi", [P, FB, T], F32R)
        act_lo = sb("act_lo", [P, FB, T], F32R)
        QK, VB, SC, PO, PW = 0, 8, 12, 15, 17
        work = sb("work", [P, 5, T])
        arena = sb("arena", [P, 6, T])
        negM = sb("negM", [HEADS, T])
        rinv = sb("rinv", [P, T])
        vec = sb("vec", [P, N_VEC])
        ident = sb("ident", [P, P])
        ones = sb("ones", [P, P])
        mask = sb("mask", [P, P])
        ones_r = sb("ones_r", [P, 2], F32R)
        sel = sb("sel", [HEADS, P])
        rcol = sb("rcol", [P, TB])
        ycol = sb("ycol", [P, TB])
        tcol = sb("tcol", [P, TB])
        acol = sb("acol", [P, TB])
        qcol = sb("qcol", [P, TB])
        dcol = sb("dcol", [P, TB])
        ccol = sb("ccol", [P, TB * HEADS])
        emcol = sb("emcol", [P, TB * HEADS])
        em2 = sb("em2", [P, TB * HEADS])

        ps = ctx.enter_context(nc.psum_tensor("ps", [P, 8, T], F32))

        gs, us = (work[:, 0], work[:, 1]), (work[:, 2], work[:, 3])
        sq, ssq = (work[:, 2], work[:, 3]), work[:, 4]
        diag = arena[:, 5]
        probs = arena[:, 0:3].rearrange("p a n -> p (a n)")[:, 0:S_COLS]
        r_diag, t1, sqn = arena[:, 3], arena[:, 4], arena[:, 5]
        p_hi = act_hi[:, SC:SC + 3].rearrange("p a n -> p (a n)")[:, 0:S_COLS]
        p_lo = act_lo[:, SC:SC + 3].rearrange("p a n -> p (a n)")[:, 0:S_COLS]
        ps_sc = ps[:, 2:5].rearrange("p a n -> p (a n)")[:, 0:S_COLS]
        ps_num, ps_col, ps_rep = ps[:, 5], ps[:, 6], ps[:, 7]

        raw_in = [sem(f"raw_in{i}") for i in range(RAWS)]
        x_in = [sem(f"x_in{i}") for i in range(KD)]
        small_in, pw_in, stored = sem("small_in"), sem("pw_in"), sem("stored")
        hi_made, lo_made, unit_used = sem("hi_made"), sem("lo_made"), sem("unit_used")
        x_new, xhi_made, xg_made = sem("x_new"), sem("xhi_made"), sem("xg_made")
        sq_made, ssq_made, ssq_zero = sem("sq_made"), sem("ssq_made"), sem("ssq_zero")
        ms_made, diag_made, rep_made, rinv_made = sem("ms_made"), sem("diag_made"), sem("rep_made"), sem("rinv_made")
        col_step = sem("col_step")
        gate_scaled, silu_made, up_scaled = sem("gate_scaled"), sem("silu_made"), sem("up_scaled")
        prod_made, act_hi_made, act_made = sem("prod_made"), sem("act_hi_made"), sem("act_made")
        u_made, conv0, conv_step, conv_done = sem("u_made"), sem("conv0"), sem("conv_step"), sem("conv_done")
        qk_silu, qk_hi_made, qk_made = sem("qk_silu"), sem("qk_hi_made"), sem("qk_made")
        g_dve, g_act, cm_made, cols_made = sem("g_dve"), sem("g_act"), sem("cm_made"), sem("cols_made")
        v_hi_made, v_made = sem("v_hi_made"), sem("v_made")
        o_scaled, o_made = sem("o_scaled"), sem("o_made")
        sel_made, r_rep, r_diag_made, e_made = sem("sel_made"), sem("r_rep"), sem("r_diag_made"), sem("e_made")
        sc_made, p_made, p_hi_made, p_split = sem("sc_made"), sem("p_made"), sem("p_hi_made"), sem("p_split")
        num_made, sqn_made, t1_made, ms_h = sem("num_made"), sem("sqn_made"), sem("t1_made"), sem("ms_h")
        hcol_step, hdiag_made, h_rep, hm_made = sem("hcol_step"), sem("hdiag_made"), sem("h_rep"), sem("hm_made")
        mix_hi_made, mix_made = sem("mix_hi_made"), sem("mix_made")
        pu_made, win_step, pool_step, pool_done = sem("pu_made"), sem("win_step"), sem("pool_step"), sem("pool_done")
        pool_hi_made, pool_made, pm_made = sem("pool_hi_made"), sem("pool_made"), sem("pm_made")
        pw_hi_made, pw_made, pmx_hi, pmx_made = sem("pw_hi_made"), sem("pw_made"), sem("pmx_hi"), sem("pmx_made")
        ones_made, y_made = sem("ones_made"), sem("y_made")

        block = ctx.enter_context(nc.Block())

        def scalar_of(col):
            return vec[:, col:col + 1]

        def f32(ap):
            return ap.bitcast(F32)

        @block.sync
        def _(sp):
            def load(n, k):
                sp.dma_start(raw[:, k % RAWS], weights[bass.ds(n, 1)].rearrange("a p n -> p (a n)")
                             ).then_inc(raw_in[k % RAWS], 16)

            for n in range(RAWS):
                load(n, n)
            loops = (N_UNITS - RAWS) // RAWS
            with sp.Fori(0, loops) as it:
                for j in range(RAWS):
                    sp.wait_ge(lo_made, it * RAWS + (j + 1))
                    load(it * RAWS + (RAWS + j), RAWS + j)
            for n in range(RAWS + loops * RAWS, N_UNITS):
                sp.wait_ge(lo_made, n - RAWS + 1)
                load(n, n)
            for d in range(KD):
                sp.wait_ge(y_made, d + 1)
                sp.dma_start(out[d * P:(d + 1) * P, :], x[:, d]).then_inc(stored, 16)
            sp.wait_ge(stored, 16 * KD)

        @block.tensor
        def _(pe):
            def three_passes(acc, hi, lo, m_hi, m_lo, first, last):
                pe.matmul(acc, hi, m_hi, start=first, stop=False)
                pe.matmul(acc, hi, m_lo, start=False, stop=False)
                return pe.matmul(acc, lo, m_hi, start=False, stop=last)

            def weight(n, tile):
                s = n % SLOTS
                return w_hi[:, s, tile * P:(tile + 1) * P], w_lo[:, s, tile * P:(tile + 1) * P]

            def column_block(n, seen, acc, ready=None, order=range(KD), m_hi=xg_hi, m_lo=xg_lo):
                pe.wait_ge(lo_made, seen + 1)
                for at, k in enumerate(order):
                    if ready is not None:
                        pe.wait_ge(*ready(k))
                    mm = three_passes(acc, *weight(n, k), m_hi[:, k], m_lo[:, k], at == 0, at == KD - 1)
                mm.then_inc(unit_used, 1)

            def mean_columns(stage):
                pe.wait_ge(ssq_made, KD * (stage + 1))
                for tb in range(TB):
                    mm = pe.matmul(ps_rep[:, tb:tb + 1], ssq[:, tb * P:(tb + 1) * P],
                                   scalar_of(V_MEAN_D), start=True, stop=True)
                mm.then_inc(ms_made, 1)

            def replicate(stage):
                pe.wait_ge(diag_made, stage + 1)
                pe.matmul(ps_rep, ones[:], diag, start=True, stop=True).then_inc(rep_made, 1)

            def ffn_up(base, p, stage):
                def step(f, j, first=False):
                    n = base + 2 * j
                    if not first or j >= 2:
                        pe.wait_ge(up_scaled, p * FB + f - 1)
                    ready = (lambda k: (xg_made, KD * stage + k + 1)) if first and j == 0 else None
                    column_block(n, f * 2 + base, ps[:, 2 * (j % 2)], ready)
                    if first and j == 0:
                        mean_columns(stage)
                    if first and j == 1:
                        replicate(stage)
                    column_block(n + 1, f * 2 + (base + 1), ps[:, 2 * (j % 2) + 1])

                step(0, 0, True)
                step(1, 1, True)
                with pe.Fori(1, FB // 2) as it:
                    step(it * 2, 2)
                    step(it * 2 + 1, 3)

            def ffn_down(base, p, out_stage):
                def step(d, j):
                    acc = ps[:, 4 + j % 2]
                    pe.wait_ge(ssq_made, d + (KD * (out_stage + 1) - 1))
                    for f in range(FB):
                        n = base + DN_UNITS * j + f // KD
                        if f == 0:
                            pe.wait_ge(act_made, p * FB + FB - 2)
                        if f == FB - 2:
                            pe.wait_ge(act_made, p * FB + FB)
                        if f % KD == 0:
                            pe.wait_ge(lo_made, d * DN_UNITS + (base + f // KD + 1))
                        mm = three_passes(acc, *weight(n, f % KD), act_hi[:, f], act_lo[:, f],
                                          f == 0, f == FB - 1)
                        if f % KD == KD - 1 or f == FB - 1:
                            mm.then_inc(unit_used, 1)

                with pe.Fori(0, KD // 4) as it:
                    for j in range(4):
                        step(it * 4 + j, j)

            def mixer():
                n = MIX
                column_block(n, n, ps[:, 2], lambda k: (xg_made, KD + k + 1))
                mean_columns(1)
                for i in range(2 * HEADS):
                    n = QK_UNIT + i
                    if i >= 2:
                        pe.wait_ge(u_made, i - 1)
                    column_block(n, n, ps[:, i % 2])
                    if i == 0:
                        replicate(1)
                pe.wait_ge(cm_made, 1)
                for what in range(2):
                    rows = arena[0:HEADS, 1 if what == 0 else 3]
                    for tb in range(TB):
                        at = 4 * (4 * what + tb)
                        mm = pe.matmul(ps[:, 3, at:at + 4], rows[:, tb * P:(tb + 1) * P],
                                       ident[0:HEADS, 0:HEADS], start=True, stop=True)
                mm.then_inc(cols_made, 1)
                pe.wait_ge(rinv_made, 2)
                for i in range(4):
                    n = V_UNIT + i
                    pe.wait_ge(lo_made, n + 1)
                    for kk in range(2):
                        k = 2 * i + kk
                        wh = w_hi[:, n % SLOTS, kk * T:(kk + 1) * T]
                        wl = w_lo[:, n % SLOTS, kk * T:(kk + 1) * T]
                        for tb in range(TB):
                            xh = xg_hi[:, k, tb * P:(tb + 1) * P]
                            xl = xg_lo[:, k, tb * P:(tb + 1) * P]
                            mm = three_passes(ps[:, 4 + tb], xh, xl, wh, wl, k == 0, k == KD - 1)
                    mm.then_inc(unit_used, 1)

                def proj(i):
                    n = O_UNIT + i
                    if i < 2:
                        pe.wait_ge(u_made, 2 * HEADS - 1 + i)
                    elif i - 2 < HEADS:
                        pe.wait_ge(o_scaled, i - 1)
                    else:
                        pe.wait_ge(pu_made, i - 2 - HEADS + 1)
                    column_block(n, n, ps[:, i % 2])

                def scores(h):
                    if h == 0:
                        pe.wait_ge(v_made, TB)
                        pe.wait_ge(cols_made, 3)
                    else:
                        pe.wait_ge(hm_made, h - 1) if h > 1 else None
                        pe.wait_ge(p_made, h)
                    pe.wait_ge(sel_made, h + 1)
                    pe.matmul(ps_rep, sel[:, :], negM[:, :], start=True, stop=True).then_inc(r_rep, 1)
                    pe.wait_ge(qk_made, 2 * h + 2)
                    for S in range(TB):
                        w = T - S * P
                        keys, queries = slice(S * P, (S + 1) * P), slice(S * P, T)
                        mm = three_passes(ps_sc[:, S_OFF[S]:S_OFF[S] + w],
                                          act_hi[:, QK + 4 + h, keys], act_lo[:, QK + 4 + h, keys],
                                          act_hi[:, QK + h, queries], act_lo[:, QK + h, queries],
                                          True, True)
                    mm.then_inc(sc_made, 1)

                def values(h):
                    pe.wait_ge(p_split, h + 1)
                    if h >= 1:
                        pe.wait_ge(t1_made, h)
                        pe.wait_ge(sqn_made, h)
                        pe.wait_ge(hdiag_made, h)
                    for S in range(TB):
                        w = T - S * P
                        v = slice(h * P, (h + 1) * P)
                        at = slice(S_OFF[S], S_OFF[S] + w)
                        mm = three_passes(ps_num[:, S * P:T], act_hi[:, VB + S, v], act_lo[:, VB + S, v],
                                          p_hi[:, at], p_lo[:, at], S == 0, S == TB - 1)
                    for tb in range(TB):
                        for S in range(tb + 1):
                            at = S_OFF[S] + (tb - S) * P
                            for part in (p_hi, p_lo):
                                mm = pe.matmul(ps_col[:, 2 * tb:2 * tb + 2], part[:, at:at + P], ones_r[:, :],
                                               start=(S == 0 and part is p_hi), stop=(S == tb and part is p_lo))
                    mm.then_inc(num_made, 1)

                def head_mean(h):
                    pe.wait_ge(sqn_made, h + 1)
                    pe.wait_ge(hcol_step, 15 * h + 1)
                    for tb in range(TB):
                        mm = pe.matmul(ps_col[:, 8 + tb:9 + tb], sqn[:, tb * P:(tb + 1) * P],
                                       scalar_of(V_MEAN_H), start=True, stop=True)
                    mm.then_inc(ms_h, 1)

                def head_rep(h):
                    pe.wait_ge(hdiag_made, h + 1)
                    pe.wait_ge(e_made, min(h + 2, HEADS))
                    pe.wait_ge(r_diag_made, min(h + 2, HEADS))
                    pe.matmul(ps_rep, ones[:], diag, start=True, stop=True).then_inc(h_rep, 1)

                def pool_mix(i):
                    g = HEADS - 1 - i
                    if i == 0:
                        pe.wait_ge(pw_made, 1)
                    pe.wait_ge(pool_made, i + 1)
                    at = slice(g * P, (g + 1) * P)
                    three_passes(ps[:, 2 + i % 2], act_hi[:, PW, at], act_lo[:, PW, at],
                                 act_hi[:, PO + i % 2], act_lo[:, PO + i % 2], True, True).then_inc(pm_made, 1)

                proj(0)
                scores(0)
                proj(1)
                values(0)
                scores(1)
                head_mean(0)
                proj(2)
                head_rep(0)
                values(1)
                scores(2)
                head_mean(1)
                proj(3)
                head_rep(1)
                values(2)
                scores(3)
                head_mean(2)
                proj(4)
                head_rep(2)
                values(3)
                head_mean(3)
                proj(5)
                head_rep(3)
                pe.wait_ge(p_made, HEADS)
                pool_mix(0)
                proj(6)
                pool_mix(1)
                proj(7)
                pe.wait_ge(pmx_made, 1)
                pool_mix(2)

                def wout(d, j, first=False):
                    n = WO_UNIT + j
                    acc = ps[:, 4 + j % 2]
                    if first:
                        pe.wait_ge(lo_made, n + 1)
                        pe.wait_ge(mix_made, HEADS)
                        order = (0, 1, 2, 3, 7, 6, 5, 4)
                        for at, k in enumerate(order):
                            if k >= HEADS:
                                if k == 4:
                                    pool_mix(3)
                                pe.wait_ge(pmx_made, 2 * HEADS - k)
                            mm = three_passes(acc, *weight(n, k), act_hi[:, QK + k], act_lo[:, QK + k],
                                              at == 0, at == KD - 1)
                        mm.then_inc(unit_used, 1)
                    else:
                        if j >= 2:
                            pe.wait_ge(x_new, KD + d - 1)
                        column_block(n, n, acc, m_hi=act_hi[:, QK:QK + KD], m_lo=act_lo[:, QK:QK + KD])

                wout(0, 0, True)
                for d in range(1, KD):
                    wout(d, d)

            pe.wait_ge(small_in, 16 * 4)
            ffn_up(UP1, 0, 0)
            ffn_down(DN1, 0, 0)
            mixer()
            ffn_up(UP2, 1, 2)
            ffn_down(DN2, 1, 2)
            mean_columns(3)
            replicate(3)

        @block.scalar
        def _(act):
            act.dma_start(vec[:], vecs).then_inc(small_in, 16)
            act.dma_start(x[:, 0], x_t[0:P]).then_inc(x_in[0], 16)
            for name, (t, i) in {"ident": (ident, 0), "ones": (ones, 1), "mask": (mask, 2)}.items():
                act.dma_start(t[:], consts[i]).then_inc(small_in, 16)
            for d in range(1, KD):
                act.dma_start(x[:, d], x_t[d * P:(d + 1) * P]).then_inc(x_in[d], 16)

            def split_hi(k, seen, loads, first=False):
                act.wait_ge(raw_in[k % RAWS], loads * 16)
                if not first:
                    act.wait_ge(unit_used, seen - (SLOTS - 1))
                act.activation(w_hi[:, k % SLOTS], raw[:, k % RAWS], ACT.Copy).then_inc(hi_made, 1)

            def prep_x(d, stage):
                if stage == 0:
                    act.wait_ge(x_in[d], 16)
                else:
                    act.wait_ge(x_new, KD * (stage - 1) + d + 1)
                if stage < 3:
                    act.activation(xg_hi[:, d], x[:, d], ACT.Copy, scale=scalar_of(V_GAIN + stage * KD + d)
                                   ).then_inc(xhi_made, 1)

            def square_x(d, stage):
                n = KD * stage + d
                if n >= 2:
                    act.wait_ge(ssq_made, n - 1)
                act.activation(sq[n % 2], x[:, d], ACT.Square).then_inc(sq_made, 1)

            def ffn_up(base, p):
                def step(f, j):
                    n = base + 2 * j
                    split_hi(n + SLOTS, f * 2 + (base + SLOTS), f + ((base + SLOTS) // 2 + 1))
                    act.wait_ge(gate_scaled, f + (p * FB + 1))
                    act.activation(gs[j % 2], gs[j % 2], ACT.Silu).then_inc(silu_made, 1)
                    split_hi(n + SLOTS + 1, f * 2 + (base + SLOTS + 1), f + ((base + SLOTS + 1) // 2 + 1))

                step(0, 0)
                step(1, 1)
                with act.Fori(1, FB // 2) as it:
                    step(it * 2, 2)
                    step(it * 2 + 1, 3)

            def out_blocks(base, per, stage):
                for d in range(KD):
                    for i in range(per):
                        n = base + per * d + SLOTS + i
                        if n < N_UNITS:
                            split_hi(n, n, n // RAWS + 1)
                    prep_x(d, stage)
                    square_x(d, stage)

            def mixer():
                nxt = [MIX + SLOTS]

                def split_next():
                    split_hi(nxt[0], nxt[0], nxt[0] // RAWS + 1)
                    nxt[0] += 1

                split_next()
                act.preload_act_table_set("natural_log_exp_and_others")
                fr = slice(32, 32 + HEADS)
                act.wait_ge(g_dve, 1)
                act.activation(arena[fr, 1], arena[fr, 0], ACT.Abs, bias=vec[fr, V_BG:V_BG + 1]).then_inc(g_act, 1)
                act.wait_ge(g_act, 1)
                act.activation(arena[fr, 1], arena[fr, 1], ACT.Exp, scale=-1.0).then_inc(g_act, 1)
                act.wait_ge(g_act, 2)
                act.activation(arena[fr, 1], arena[fr, 1], ACT.Ln, bias=ones[fr, 0:1]).then_inc(g_act, 1)
                for i in range(2 * HEADS):
                    h, is_k = i // 2, i % 2
                    b = h + HEADS * is_k
                    split_next()
                    act.wait_ge(u_made, i + 1)
                    if i >= 2:
                        act.wait_ge(qk_made, i - 1)
                    act.activation(work[:, 2 + i % 2], work[:, i % 2], ACT.Identity,
                                   bias=scalar_of(V_CONVB + b), scale=scalar_of(V_CONVW + 4 * b + 3)
                                   ).then_inc(conv0, 1)
                    act.wait_ge(conv_done, i + 1)
                    act.activation(work[:, 2 + i % 2], work[:, 2 + i % 2], ACT.Silu).then_inc(qk_silu, 1)
                    act.wait_ge(qk_silu, i + 1)
                    act.activation(act_hi[:, QK + b], work[:, 2 + i % 2], ACT.Copy,
                                   scale=K_SCALE if is_k else 1.0).then_inc(qk_hi_made, 1)
                act.wait_ge(pw_in, 16)
                act.activation(act_hi[:, PW], arena[:, 4], ACT.Copy).then_inc(pw_hi_made, 1)
                act.wait_ge(cols_made, 1)
                act.activation(emcol[:], ps[:, 3, 16:32], ACT.Exp, scale=-1.0).then_inc(cols_made, 1)
                for i in range(4):
                    split_next()
                for tb in range(TB):
                    act.wait_ge(unit_used, V_UNIT + 4)
                    act.activation(act_hi[:, VB + tb], ps[:, 4 + tb], ACT.Copy, scale=rcol[:, tb:tb + 1]
                                   ).then_inc(v_hi_made, 1)

                def gate(h):
                    act.wait_ge(o_scaled, h + 1)
                    act.activation(work[:, h % 2], work[:, h % 2], ACT.Sigmoid).then_inc(o_made, 1)

                def weights_of(h):
                    act.wait_ge(r_diag_made, h + 1)
                    if h == 0:
                        act.wait_ge(cols_made, 3)
                    else:
                        act.wait_ge(p_split, h)
                    for S in range(TB - 1):
                        act.activation(probs[:, S_OFF[S] + P:S_OFF[S] + T - S * P],
                                       ps_rep[:, (S + 1) * P:T], ACT.Exp,
                                       bias=ccol[:, 4 * S + h:4 * S + h + 1])
                    for S in range(TB):
                        ins = act.activation(probs[:, S_OFF[S]:S_OFF[S] + P], r_diag[:, S * P:(S + 1) * P],
                                             ACT.Exp, bias=ccol[:, 4 * S + h:4 * S + h + 1])
                    ins.then_inc(e_made, 1)

                def probs_hi(h):
                    act.wait_ge(p_made, h + 1)
                    if h >= 1:
                        act.wait_ge(num_made, h)
                    act.activation(p_hi, probs, ACT.Copy).then_inc(p_hi_made, 1)

                def square_num(h):
                    act.wait_ge(num_made, h + 1)
                    if h >= 1:
                        act.wait_ge(h_rep, h)
                    act.activation(sqn, ps_num, ACT.Square).then_inc(sqn_made, 1)

                def mixed_hi(h):
                    act.wait_ge(hm_made, h + 1)
                    act.activation(act_hi[:, QK + h], t1, ACT.Copy).then_inc(mix_hi_made, 1)

                def pool_hi(i):
                    act.wait_ge(pool_done, i + 1)
                    if i >= 2:
                        act.wait_ge(pm_made, i - 1)
                    act.activation(act_hi[:, PO + i % 2], work[:, 3 + (HEADS - i) % 2], ACT.Copy).then_inc(pool_hi_made, 1)

                def pool_mixed_hi(i):
                    g = HEADS - 1 - i
                    act.wait_ge(pm_made, i + 1)
                    act.activation(act_hi[:, QK + HEADS + g], ps[:, 2 + i % 2], ACT.Copy,
                                   scale=scalar_of(V_PSC + g)).then_inc(pmx_hi, 1)

                gate(0)
                weights_of(0)
                split_next()
                probs_hi(0)
                gate(1)
                split_next()
                square_num(0)
                weights_of(1)
                probs_hi(1)
                gate(2)
                split_next()
                mixed_hi(0)
                square_num(1)
                weights_of(2)
                probs_hi(2)
                gate(3)
                split_next()
                mixed_hi(1)
                square_num(2)
                weights_of(3)
                probs_hi(3)
                split_next()
                mixed_hi(2)
                square_num(3)
                split_next()
                mixed_hi(3)
                pool_hi(0)
                pool_mixed_hi(0)
                split_next()
                pool_hi(1)
                pool_mixed_hi(1)
                split_next()
                pool_hi(2)
                pool_mixed_hi(2)
                pool_hi(3)
                pool_mixed_hi(3)
                assert nxt[0] <= WO_UNIT + SLOTS
                while nxt[0] < WO_UNIT + SLOTS:
                    split_next()

            act.wait_ge(small_in, 16 * 4)
            split_hi(0, 0, 1, True)
            for d in range(KD):
                if d == 3:
                    split_hi(1, 1, 1, True)
                prep_x(d, 0)
            square_x(0, 0)
            square_x(1, 0)
            split_hi(2, 2, 2, True)
            for d in range(2, KD):
                square_x(d, 0)
            split_hi(3, 3, 2, True)
            ffn_up(UP1, 0)
            out_blocks(DN1, DN_UNITS, 1)
            mixer()
            out_blocks(WO_UNIT, 1, 2)
            ffn_up(UP2, 1)
            out_blocks(DN2, DN_UNITS, 3)

        @block.gpsimd
        def _(pool):
            pool.dma_start(arena[:, 4], pool_w).then_inc(pw_in, 16)
            win = 0
            for i in range(HEADS):
                g = HEADS - 1 - i
                pool.wait_ge(pu_made, i + 1)
                src = work[:, 2]
                for s in range(g + 1):
                    dst = work[:, 3 + s % 2]
                    sh = 1 << s
                    if s > 0:
                        pool.wait_ge(win_step, win)
                    pool.tensor_copy(dst[:, 0:sh], src[:, 0:sh])
                    pool.tensor_tensor(dst[:, sh:T], src[:, sh:T], src[:, 0:T - sh], ALU.add).then_inc(win_step, 1)
                    win += 1
                    src = dst

        @block.vector
        def _(dve):
            def split_lo(k, seen):
                dve.wait_ge(hi_made, seen + 1)
                dve.tensor_tensor(w_lo[:, k % SLOTS], raw[:, k % RAWS], f32(w_hi[:, k % SLOTS]),
                                  ALU.subtract).then_inc(lo_made, 1)

            def split_xg(d, stage):
                dve.wait_ge(xhi_made, KD * stage + d + 1)
                dve.scalar_tensor_tensor(xg_lo[:, d], x[:, d], scalar_of(V_GAIN + stage * KD + d),
                                         f32(xg_hi[:, d]), ALU.mult, ALU.subtract).then_inc(xg_made, 1)

            def add_square(d, stage):
                n = KD * stage + d
                dve.wait_ge(sq_made, n + 1)
                if d == 0:
                    dve.wait_ge(ssq_zero, stage + 1)
                else:
                    dve.wait_ge(ssq_made, n)
                dve.tensor_tensor(ssq, ssq, sq[n % 2], ALU.add).then_inc(ssq_made, 1)

            def clear_squares(stage):
                if stage:
                    dve.wait_ge(ms_made, stage)
                dve.memset(ssq, 0.0).then_inc(ssq_zero, 1)

            def rsqrt(step, count):
                def then(ins):
                    nonlocal count
                    ins.then_inc(step, 1)
                    count += 1
                    dve.wait_ge(step, count)

                then(dve.tensor_scalar(ycol[:].bitcast(I32), acol[:].bitcast(I32), 1, None, ALU.logical_shift_right))
                then(dve.tensor_scalar(ycol[:].bitcast(I32), ycol[:].bitcast(I32), -1.0, RSQRT_SEED, ALU.mult, ALU.add))
                for _ in range(3):
                    then(dve.scalar_tensor_tensor(tcol[:], ycol[:], -0.5, acol[:], ALU.mult, ALU.mult))
                    then(dve.tensor_tensor(tcol[:], tcol[:], ycol[:], ALU.mult))
                    then(dve.scalar_tensor_tensor(ycol[:], tcol[:], 1.5, ycol[:], ALU.add, ALU.mult))
                return count

            def make_diag(signal):
                for tb in range(TB):
                    ins = dve.tensor_scalar(diag[:, tb * P:(tb + 1) * P], ident[:], ycol[:, tb:tb + 1], None, ALU.mult)
                ins.then_inc(signal, 1)

            STEPS = 12

            def inverse_rms(stage):
                base = STEPS * stage
                dve.wait_ge(ms_made, stage + 1)
                dve.tensor_scalar(acol[:], ps_rep[:, 0:TB], EPS, None, ALU.add).then_inc(col_step, 1)
                dve.wait_ge(col_step, base + 1)
                done = rsqrt(col_step, base + 1)
                assert done == base + STEPS
                if stage == 1:
                    dve.tensor_copy(rcol[:], ycol[:])
                make_diag(diag_made)

            def take_rinv(stage):
                dve.wait_ge(rep_made, stage + 1)
                dve.tensor_copy(rinv[:], ps_rep).then_inc(rinv_made, 1)
                dve.wait_ge(rinv_made, stage + 1)

            def ffn_up(base, p):
                def step(f, j):
                    n = base + 2 * j
                    g, u = gs[j % 2], us[j % 2]
                    G, U = ps[:, 2 * (j % 2)], ps[:, 2 * (j % 2) + 1]
                    dve.wait_ge(unit_used, f * 2 + (base + 2))
                    dve.tensor_tensor(g, G, rinv[:], ALU.mult).then_inc(gate_scaled, 1)
                    dve.tensor_tensor(u, U, rinv[:], ALU.mult).then_inc(up_scaled, 1)
                    split_lo(n + SLOTS, f * 2 + (base + SLOTS))
                    dve.wait_ge(silu_made, f + (p * FB + 1))
                    dve.wait_ge(up_scaled, f + (p * FB + 1))
                    dve.tensor_tensor(u, u, g, ALU.mult).then_inc(prod_made, 1)
                    split_lo(n + SLOTS + 1, f * 2 + (base + SLOTS + 1))
                    hi = act_hi[:, bass.ds(f, 1)].rearrange("p a n -> p (a n)")
                    lo = act_lo[:, bass.ds(f, 1)].rearrange("p a n -> p (a n)")
                    dve.wait_ge(prod_made, f + (p * FB + 1))
                    dve.tensor_scalar(hi, u, 1.0, None, ALU.mult).then_inc(act_hi_made, 1)
                    dve.wait_ge(act_hi_made, f + (p * FB + 1))
                    dve.tensor_tensor(lo, u, f32(hi), ALU.subtract).then_inc(act_made, 1)

                step(0, 0)
                step(1, 1)
                with dve.Fori(1, FB // 2) as it:
                    step(it * 2, 2)
                    step(it * 2 + 1, 3)

            def out_blocks(base, per, stage, factor):
                for d in range(KD):
                    n = base + per * d
                    for i in range(per - 1):
                        if n + SLOTS + i < N_UNITS:
                            split_lo(n + SLOTS + i, n + SLOTS + i)
                    dve.wait_ge(unit_used, n + per)
                    dve.scalar_tensor_tensor(x[:, d], ps[:, 4 + d % 2], factor, x[:, d],
                                             ALU.mult, ALU.add).then_inc(x_new, 1)
                    if n + SLOTS + per - 1 < N_UNITS:
                        split_lo(n + SLOTS + per - 1, n + SLOTS + per - 1)
                    if stage < 3:
                        dve.wait_ge(x_new, KD * (stage - 1) + d + 1)
                        split_xg(d, stage)
                    add_square(d, stage)

            def mixer():
                nxt = [MIX + SLOTS]

                def split_next():
                    split_lo(nxt[0], nxt[0])
                    nxt[0] += 1

                inverse_rms(1)
                take_rinv(1)
                split_next()
                R = slice(0, HEADS)
                fr = slice(32, 32 + HEADS)
                gsc, lf = arena[:, 0], arena[:, 2]
                dve.tensor_tensor(arena[0:36, 0], ps[0:36, 2], rinv[0:36, :], ALU.mult).then_inc(g_dve, 1)
                dve.wait_ge(g_dve, 1)
                dve.tensor_scalar(lf[fr], gsc[fr], vec[fr, V_BG:V_BG + 1], 0.0, ALU.add, ALU.min).then_inc(g_dve, 1)
                dve.tensor_scalar(gsc[R], gsc[R], vec[R, V_BG:V_BG + 1], None, ALU.add).then_inc(g_dve, 1)

                def gates():
                    count = [3]

                    def then(ins):
                        count[0] += 1
                        ins.then_inc(g_dve, 1)
                        dve.wait_ge(g_dve, count[0])

                    dve.wait_ge(g_dve, 3)
                    dve.wait_ge(g_act, 3)
                    then(dve.tensor_tensor(lf[fr], lf[fr], arena[fr, 1], ALU.subtract))
                    then(dve.tensor_copy(lf[R], lf[fr]))
                    B, m = arena[R, 1], arena[R, 3]
                    then(dve.tensor_tensor_scan(B, lf[R], lf[R], 0.0, ALU.add, ALU.min))
                    then(dve.tensor_tensor(B, gsc[R], B, ALU.subtract))
                    then(dve.tensor_tensor_scan(negM[:, :], B, B, 0.0, ALU.max, ALU.max))
                    then(dve.tensor_scalar(negM[:, :], negM[:, :], -1.0, None, ALU.mult))
                    dve.tensor_tensor_scan(m, lf[R], gsc[R], 0.0, ALU.add, ALU.max).then_inc(cm_made, 1)
                    dve.tensor_scalar(sel[:, :], ones[R, :], ident[R, 0:1], None, ALU.mult).then_inc(sel_made, 1)

                for i in range(2 * HEADS):
                    h, is_k = i // 2, i % 2
                    b = h + HEADS * is_k
                    u, a = work[:, i % 2], work[:, 2 + i % 2]
                    dve.wait_ge(unit_used, QK_UNIT + i + 1)
                    if i >= 2:
                        dve.wait_ge(conv0, i - 1)
                    dve.tensor_tensor(u, ps[:, i % 2], rinv[:], ALU.mult).then_inc(u_made, 1)
                    split_next()
                    dve.wait_ge(u_made, i + 1)
                    dve.wait_ge(conv0, i + 1)
                    for back in range(1, 4):
                        ins = dve.scalar_tensor_tensor(a[:, back:T], u[:, 0:T - back],
                                                       scalar_of(V_CONVW + 4 * b + 3 - back), a[:, back:T],
                                                       ALU.mult, ALU.add)
                        if back < 3:
                            ins.then_inc(conv_step, 1)
                            dve.wait_ge(conv_step, 2 * i + back)
                    ins.then_inc(conv_done, 1)
                    if i == 0:
                        gates()
                    dve.wait_ge(qk_hi_made, i + 1)
                    dve.scalar_tensor_tensor(act_lo[:, QK + b], a, K_SCALE if is_k else 1.0,
                                             f32(act_hi[:, QK + b]), ALU.mult, ALU.subtract).then_inc(qk_made, 1)
                dve.wait_ge(pw_hi_made, 1)
                dve.tensor_tensor(act_lo[:, PW], arena[:, 4], f32(act_hi[:, PW]), ALU.subtract).then_inc(pw_made, 1)
                dve.wait_ge(cols_made, 2)
                dve.tensor_copy(ccol[:], ps[:, 3, 0:16]).then_inc(cols_made, 1)
                dve.scalar_tensor_tensor(em2[:], emcol[:], EPS, emcol[:], ALU.mult, ALU.mult).then_inc(cols_made, 1)
                for i in range(4):
                    split_next()
                for tb in range(TB):
                    dve.wait_ge(v_hi_made, tb + 1)
                    dve.scalar_tensor_tensor(act_lo[:, VB + tb], ps[:, 4 + tb], rcol[:, tb:tb + 1],
                                             f32(act_hi[:, VB + tb]), ALU.mult, ALU.subtract).then_inc(v_made, 1)

                def gate(h):
                    dve.wait_ge(unit_used, O_UNIT + h + 1)
                    if h >= 2:
                        dve.wait_ge(t1_made, h - 1)
                    dve.tensor_tensor(work[:, h % 2], ps[:, h % 2], rinv[:], ALU.mult).then_inc(o_scaled, 1)

                def next_sel(h):
                    dve.wait_ge(r_rep, h)
                    dve.tensor_scalar(sel[:, :], ones[R, :], ident[R, h:h + 1], None, ALU.mult).then_inc(sel_made, 1)

                def masked(h):
                    dve.wait_ge(r_rep, h + 1)
                    if h >= 1:
                        dve.wait_ge(e_made, h)
                    for S in range(TB):
                        at = slice(S * P, (S + 1) * P)
                        ins = dve.tensor_tensor(r_diag[:, at], ps_rep[:, at], mask[:], ALU.add)
                    ins.then_inc(r_diag_made, 1)

                def probs_of(h):
                    dve.wait_ge(sc_made, h + 1)
                    dve.wait_ge(e_made, h + 1)
                    dve.tensor_tensor(probs, probs, ps_sc, ALU.mult).then_inc(p_made, 1)

                def probs_lo(h):
                    dve.wait_ge(p_made, h + 1)
                    dve.wait_ge(p_hi_made, h + 1)
                    dve.tensor_tensor(p_lo, probs, f32(p_hi), ALU.subtract).then_inc(p_split, 1)

                def head_scale(h):
                    dve.wait_ge(num_made, h + 1)
                    count = (STEPS + 3) * h

                    def then(ins):
                        nonlocal count
                        ins.then_inc(hcol_step, 1)
                        count += 1
                        dve.wait_ge(hcol_step, count)

                    then(dve.tensor_copy(qcol[:], ps_col[:, 0:8:2]))
                    then(dve.scalar_tensor_tensor(dcol[:], qcol[:], EPS, qcol[:], ALU.mult, ALU.mult))
                    if h == 0:
                        dve.wait_ge(cols_made, 4)
                    then(dve.tensor_tensor(dcol[:], dcol[:], em2[:, h:16:4], ALU.max))
                    dve.wait_ge(sqn_made, h + 1)
                    dve.wait_ge(o_made, h + 1)
                    if h >= 1:
                        dve.wait_ge(mix_made, h)
                    dve.scalar_tensor_tensor(t1, ps_num, scalar_of(V_MH + h), work[:, h % 2],
                                             ALU.mult, ALU.mult).then_inc(t1_made, 1)

                def head_rsqrt(h):
                    count = (STEPS + 3) * h + 3
                    dve.wait_ge(ms_h, h + 1)
                    dve.scalar_tensor_tensor(acol[:], ps_col[:, 8:8 + TB], TINY, dcol[:],
                                             ALU.add, ALU.add).then_inc(hcol_step, 1)
                    dve.wait_ge(hcol_step, count + 1)
                    rsqrt(hcol_step, count + 1)
                    make_diag(hdiag_made)

                def mixed(h):
                    dve.wait_ge(h_rep, h + 1)
                    dve.tensor_tensor(t1, t1, ps_rep, ALU.mult).then_inc(hm_made, 1)

                def mixed_lo(h):
                    dve.wait_ge(hm_made, h + 1)
                    dve.wait_ge(mix_hi_made, h + 1)
                    dve.tensor_tensor(act_lo[:, QK + h], t1, f32(act_hi[:, QK + h]),
                                      ALU.subtract).then_inc(mix_made, 1)

                def pool_in(i):
                    dve.wait_ge(unit_used, PL_UNIT + i + 1)
                    if i >= 1:
                        dve.wait_ge(pool_made, i)
                    dve.tensor_tensor(work[:, 2], ps[:, i % 2], rinv[:], ALU.mult).then_inc(pu_made, 1)

                def pool_mean(i):
                    g = HEADS - 1 - i
                    s, dst = work[:, 3 + g % 2], work[:, 3 + (HEADS - i) % 2]
                    dve.wait_ge(win_step, sum(HEADS - k for k in range(i + 1)))
                    dve.wait_ge(pu_made, i + 1)
                    inv = vec[:, V_INV + MAXWIN * g:V_INV + MAXWIN * (g + 1)]
                    dve.scalar_tensor_tensor(dst[:, MAXWIN:T], s[:, MAXWIN:T], 1.0 / WINDOWS[g], work[:, 2, MAXWIN:T],
                                             ALU.mult, ALU.subtract).then_inc(pool_step, 1)
                    dve.tensor_tensor(dst[:, 0:MAXWIN], s[:, 0:MAXWIN], inv, ALU.mult).then_inc(pool_step, 1)
                    dve.wait_ge(pool_step, 2 * i + 2)
                    dve.tensor_tensor(dst[:, 0:MAXWIN], dst[:, 0:MAXWIN], work[:, 2, 0:MAXWIN],
                                      ALU.subtract).then_inc(pool_done, 1)

                def pool_lo(i):
                    dve.wait_ge(pool_done, i + 1)
                    dve.wait_ge(pool_hi_made, i + 1)
                    dve.tensor_tensor(act_lo[:, PO + i % 2], work[:, 3 + (HEADS - i) % 2], f32(act_hi[:, PO + i % 2]),
                                      ALU.subtract).then_inc(pool_made, 1)

                def pool_mixed_lo(i):
                    g = HEADS - 1 - i
                    dve.wait_ge(pmx_hi, i + 1)
                    dve.scalar_tensor_tensor(act_lo[:, QK + HEADS + g], ps[:, 2 + i % 2], scalar_of(V_PSC + g),
                                             f32(act_hi[:, QK + HEADS + g]), ALU.mult, ALU.subtract
                                             ).then_inc(pmx_made, 1)

                gate(0)
                masked(0)
                split_next()
                probs_of(0)
                probs_lo(0)
                next_sel(1)
                gate(1)
                split_next()
                for h in range(HEADS):
                    if h == HEADS - 1:
                        pool_in(0)
                    head_scale(h)
                    if h + 1 < HEADS:
                        masked(h + 1)
                    head_rsqrt(h)
                    if h + 1 < HEADS:
                        probs_of(h + 1)
                        probs_lo(h + 1)
                    if h + 2 < HEADS:
                        next_sel(h + 2)
                        gate(h + 2)
                    split_next()
                    mixed(h)
                    mixed_lo(h)
                for i in range(HEADS):
                    pool_mean(i)
                    pool_lo(i)
                    if i + 1 < HEADS:
                        pool_in(i + 1)
                    pool_mixed_lo(i)
                    if i < 2:
                        split_next()
                clear_squares(2)
                assert nxt[0] == WO_UNIT + SLOTS

            dve.memset(f32(ones_r[:]), 1.0).then_inc(ones_made, 1)
            clear_squares(0)
            dve.wait_ge(small_in, 16 * 4)
            split_lo(0, 0)
            for d in range(KD):
                split_xg(d, 0)
                if d == 3:
                    split_lo(1, 1)
            add_square(0, 0)
            add_square(1, 0)
            split_lo(2, 2)
            for d in range(2, KD):
                add_square(d, 0)
            split_lo(3, 3)
            inverse_rms(0)
            take_rinv(0)
            clear_squares(1)
            ffn_up(UP1, 0)
            out_blocks(DN1, DN_UNITS, 1, 0.5)
            mixer()
            out_blocks(WO_UNIT, 1, 2, 1.0)
            inverse_rms(2)
            take_rinv(2)
            clear_squares(3)
            ffn_up(UP2, 1)
            out_blocks(DN2, DN_UNITS, 3, 0.5)
            inverse_rms(3)
            dve.wait_ge(rep_made, 4)
            for d in range(KD):
                dve.scalar_tensor_tensor(x[:, d], x[:, d], scalar_of(V_GAIN + 3 * KD + d), ps_rep,
                                         ALU.mult, ALU.mult).then_inc(y_made, 1)


def _blocks(w):
    rows, cols = w.shape
    return w.reshape(rows // P, P, cols // P, P).transpose(2, 1, 0, 3).reshape(cols // P, P, rows)


def kernel(**inputs):
    import concourse.bacc as bacc
    from concourse.bass_utils import run_bass_kernel_spmd

    a = {k: np.asarray(v) for k, v in inputs.items()}

    def ffn(p):
        gate, up = _blocks(a[p + "_w_gate"][0]), _blocks(a[p + "_w_up"][0])
        yield np.stack([gate, up], 1).reshape(2 * FB, P, UNIT)
        down = np.zeros((KD, P, DN_UNITS, UNIT), np.float32)
        down.reshape(KD, P, DN_UNITS * UNIT)[:, :, :FF] = _blocks(a[p + "_w_down"][0])
        yield down.transpose(0, 2, 1, 3).reshape(DN_UNITS * KD, P, UNIT)

    def mixer():
        w = a["w_in"][0]
        half = D // 2
        gates = np.zeros((D, P), np.float32)
        gates[:, 0:HEADS] = w[:, 4 * half:4 * half + HEADS]
        gates[:, 32:32 + HEADS] = w[:, 4 * half + HEADS:4 * half + 2 * HEADS]
        yield _blocks(gates)
        q, k = _blocks(w[:, 0:half]), _blocks(w[:, half:2 * half])
        yield np.stack([q, k], 1).reshape(2 * HEADS, P, UNIT)
        v = w[:, 2 * half:3 * half].reshape(4, 2, P, half)
        yield v.transpose(0, 2, 1, 3).reshape(4, P, UNIT)
        yield _blocks(w[:, 3 * half:4 * half])
        yield _blocks(w[:, 4 * half + 2 * HEADS:])[::-1]
        yield _blocks(a["w_out"][0])

    weights = np.concatenate([*ffn("ffn1"), *mixer(), *ffn("ffn2")])
    pool_w = a["pool_w"][0].transpose(1, 0, 2).reshape(P, HEADS * P)

    vecs = np.zeros((P, N_VEC), np.float32)

    def columns(at, v):
        vecs[:, at:at + v.size // P] = v.reshape(-1, P).T

    for i, g in enumerate((a["ffn1_norm"][0], a["mix_norm"][0], a["ffn2_norm"][0], a["final_norm"])):
        columns(V_GAIN + KD * i, g)
    vecs[:, V_CONVW:V_CONVB] = a["conv_w"][0].reshape(4, KD, P).transpose(2, 1, 0).reshape(P, 4 * KD)
    columns(V_CONVB, a["conv_b"][0])
    columns(V_MH, a["mh_norm"][0])
    columns(V_PSC, a["pool_scale"][0])
    vecs[0:HEADS, V_BG] = a["b_gates"][0, 0:HEADS]
    vecs[32:32 + HEADS, V_BG] = a["b_gates"][0, HEADS:]
    vecs[:, V_MEAN_D], vecs[:, V_MEAN_H] = 1.0 / D, 1.0 / P
    for g, win in enumerate(WINDOWS):
        at = V_INV + MAXWIN * g
        vecs[:, at:at + MAXWIN] = (1.0 / np.minimum(np.arange(1, MAXWIN + 1), win)).astype(np.float32)
    causal = np.arange(P)[:, None] <= np.arange(P)[None, :]
    consts = np.stack([np.eye(P), np.ones((P, P)), np.where(causal, 0.0, -1e30)]).astype(np.float32)

    arrays = {"weights": weights, "pool_w": pool_w, "x_t": a["x"][0].T, "vecs": vecs, "consts": consts}
    arrays = {k: np.ascontiguousarray(v) for k, v in arrays.items()}
    nc = bacc.Bacc("TRN2", target_bir_lowering=False, num_devices=1)
    args = [nc.dram_tensor(k, v.shape, F32, kind="ExternalInput").ap() for k, v in arrays.items()]
    out = nc.dram_tensor("out", (D, T), F32, kind="ExternalOutput").ap()
    build_layer(nc, *args, out)
    r = run_bass_kernel_spmd(nc, [arrays], core_ids=[0])
    return np.ascontiguousarray(r.results[0]["out"].T).reshape(1, T, D)
```

```python
from contextlib import ExitStack

import numpy as np

import concourse.bass as bass
from concourse import mybir

F32 = mybir.dt.float32
F32R = mybir.dt.float32r
I32 = mybir.dt.int32
ALU = mybir.AluOpType
ACT = mybir.ActivationFunctionType

P = 128
T = 512
D = 1024
KD = D // P
FF = 2816
FB = FF // P
HEADS = 4
TB = T // P
EPS = 1e-6
K_SCALE = float(P) ** -0.5
WINDOWS = (2, 4, 8, 16)
MAXWIN = 16
TINY = 1e-37
RSQRT_SEED = float(0x5F3759DF)

UNIT = 8 * P
SLOTS = 4
RAWS = 2
DN_UNITS = 3
UP1 = 0
DN1 = UP1 + 2 * FB
MIX = DN1 + DN_UNITS * KD
QK_UNIT = MIX + 1
V_UNIT = QK_UNIT + 2 * HEADS
O_UNIT = V_UNIT + 4
PL_UNIT = O_UNIT + HEADS
WO_UNIT = PL_UNIT + HEADS
UP2 = WO_UNIT + KD
DN2 = UP2 + 2 * FB
N_UNITS = DN2 + DN_UNITS * KD

WARMUPS = 3
STEPS = 12
HSTEPS = STEPS + 3

V_GAIN = 0
V_CONVW = V_GAIN + 4 * KD
V_CONVB = V_CONVW + 4 * KD
V_MH = V_CONVB + KD
V_PSC = V_MH + HEADS
V_BG = V_PSC + HEADS
V_MEAN_D = V_BG + 1
V_MEAN_H = V_MEAN_D + 1
V_INV = V_MEAN_H + 1
N_VEC = V_INV + HEADS * MAXWIN

S_OFF = {0: 0, 1: 512, 3: 896, 2: 1024}
S_COLS = 1280


def build_layer(nc, weights, pool_w, x_t, vecs, consts, out):
    ctx = ExitStack()
    with ctx:
        def sb(name, shape, dt=F32):
            return ctx.enter_context(nc.sbuf_tensor(name, shape, dt))

        def sem(name):
            return ctx.enter_context(nc.semaphore(name))

        raw = sb("raw", [P, RAWS, UNIT])
        w_hi = sb("w_hi", [P, SLOTS, UNIT], F32R)
        w_lo = sb("w_lo", [P, SLOTS, UNIT], F32R)
        x = sb("x", [P, KD, T])
        xg_hi = sb("xg_hi", [P, KD, T], F32R)
        xg_lo = sb("xg_lo", [P, KD, T], F32R)
        act_hi = sb("act_hi", [P, FB, T], F32R)
        act_lo = sb("act_lo", [P, FB, T], F32R)
        QK, VB, SC, PO, PW, NM, SEL = 0, 8, 12, 15, 17, 18, 19
        work = sb("work", [P, 5, T])
        arena = sb("arena", [P, 6, T])
        rinv = sb("rinv", [P, T])
        vec = sb("vec", [P, N_VEC])
        ident = sb("ident", [P, P])
        ones = sb("ones", [P, P])
        mask = sb("mask", [P, P])
        ones_r = sb("ones_r", [P, 2], F32R)
        rcol = sb("rcol", [P, TB])
        ycol = sb("ycol", [P, TB])
        tcol = sb("tcol", [P, TB])
        acol = sb("acol", [P, TB])
        qcol = sb("qcol", [P, TB])
        dcol = sb("dcol", [P, TB])
        ccol = sb("ccol", [P, TB * HEADS])
        emcol = sb("emcol", [P, TB * HEADS])
        em2 = sb("em2", [P, TB * HEADS])

        ps = ctx.enter_context(nc.psum_tensor("ps", [P, 8, T], F32))

        gs, us = (work[:, 0], work[:, 1]), (work[:, 2], work[:, 3])
        sq, ssq = (work[:, 2], work[:, 3]), work[:, 4]
        diag = arena[:, 5]
        probs = arena[:, 0:3].rearrange("p a n -> p (a n)")[:, 0:S_COLS]
        r_diag, t1, sqn = arena[:, 3], arena[:, 4], arena[:, 5]
        r_all = (work[:, 4], work[:, 3])
        gate_of = (work[:, 0], work[:, 1])
        pool_u = (work[:, 2], work[:, 0])
        pool_sums = ((work[:, 3], work[:, 4]), (arena[:, 0], arena[:, 1]))
        neg_m = (act_hi[0:HEADS, NM], act_lo[0:HEADS, NM])
        sel = act_hi[0:HEADS, SEL]
        p_hi = act_hi[:, SC:SC + 3].rearrange("p a n -> p (a n)")[:, 0:S_COLS]
        p_lo = act_lo[:, SC:SC + 3].rearrange("p a n -> p (a n)")[:, 0:S_COLS]
        ps_sc = ps[:, 2:5].rearrange("p a n -> p (a n)")[:, 0:S_COLS]
        ps_num, ps_col, ps_rep = ps[:, 5], ps[:, 6], ps[:, 7]
        qk_bank = (5, 0, 4, 1)
        v_bank = (5, 6, 7, 0)
        r_bank = (7, 2, 7, 7)

        def proj_bank(i):
            return (1 + i) % 2

        raw_in = [sem(f"raw_in{i}") for i in range(RAWS)]
        x_in = [sem(f"x_in{i}") for i in range(KD)]
        first_in = [sem(f"first_in{i}") for i in range(3)]
        vec_in, const_in, pw_in, stored = sem("vec_in"), sem("const_in"), sem("pw_in"), sem("stored")
        first_hi, first_lo = sem("first_hi"), sem("first_lo")
        hi_made, lo_made, unit_used = sem("hi_made"), sem("lo_made"), sem("unit_used")
        x_new, xhi_made, xg_made = sem("x_new"), sem("xhi_made"), sem("xg_made")
        sq_made, ssq_made, ssq_zero = sem("sq_made"), sem("ssq_made"), sem("ssq_zero")
        ms_made, diag_made, rep_made, rinv_made = sem("ms_made"), sem("diag_made"), sem("rep_made"), sem("rinv_made")
        col_step = sem("col_step")
        gate_scaled, silu_made, up_scaled = sem("gate_scaled"), sem("silu_made"), sem("up_scaled")
        prod_made, act_hi_made, act_made = sem("prod_made"), sem("act_hi_made"), sem("act_made")
        u_made, conv0, conv_step, conv_done = sem("u_made"), sem("conv0"), sem("conv_step"), sem("conv_done")
        qk_silu, qk_hi_made, qk_made = sem("qk_silu"), sem("qk_hi_made"), sem("qk_made")
        g_dve, g_act, cm_made, cols_made = sem("g_dve"), sem("g_act"), sem("cm_made"), sem("cols_made")
        v_hi_made, v_made = sem("v_hi_made"), sem("v_made")
        o_scaled, o_made = sem("o_scaled"), sem("o_made")
        r_rep, r_copied, r_diag_made, e_made = sem("r_rep"), sem("r_copied"), sem("r_diag_made"), sem("e_made")
        sc_made, p_made, p_hi_made, p_split = sem("sc_made"), sem("p_made"), sem("p_hi_made"), sem("p_split")
        num_made, sqn_made, t1_made, ms_h = sem("num_made"), sem("sqn_made"), sem("t1_made"), sem("ms_h")
        hcol_step, hdiag_made, h_rep, hm_made = sem("hcol_step"), sem("hdiag_made"), sem("h_rep"), sem("hm_made")
        mix_hi_made, mix_made = sem("mix_hi_made"), sem("mix_made")
        pu_made, win_step, pool_step, pool_done = sem("pu_made"), sem("win_step"), sem("pool_step"), sem("pool_done")
        pool_hi_made, pool_made, pm_made = sem("pool_hi_made"), sem("pool_made"), sem("pm_made")
        pw_hi_made, pw_made, pmx_hi, pmx_made = sem("pw_hi_made"), sem("pw_made"), sem("pmx_hi"), sem("pmx_made")
        ones_made, y_made = sem("ones_made"), sem("y_made")

        block = ctx.enter_context(nc.Block())

        def scalar_of(col):
            return vec[:, col:col + 1]

        def f32(ap):
            return ap.bitcast(F32)

        @block.sync
        def _(sp):
            def load(n, k):
                sp.dma_start(raw[:, k % RAWS], weights[bass.ds(n, 1)].rearrange("a p n -> p (a n)")
                             ).then_inc(raw_in[k % RAWS], 16)

            for i in range(4):
                part = slice(2 * P * i, 2 * P * (i + 1))
                sp.dma_start(raw[:, 0, part], weights[0, :, part]).then_inc(first_in[i] if i < 3 else raw_in[0], 16)
            load(1, 1)
            loops = (N_UNITS - RAWS) // RAWS
            with sp.Fori(0, loops) as it:
                for j in range(RAWS):
                    sp.wait_ge(lo_made, it * RAWS + (j + 1))
                    load(it * RAWS + (RAWS + j), RAWS + j)
            for n in range(RAWS + loops * RAWS, N_UNITS):
                sp.wait_ge(lo_made, n - RAWS + 1)
                load(n, n)
            for d in range(KD):
                sp.wait_ge(y_made, d + 1)
                sp.dma_start(out[d * P:(d + 1) * P, :], x[:, d]).then_inc(stored, 16)
            sp.wait_ge(stored, 16 * KD)

        @block.tensor
        def _(pe):
            def three_passes(acc, hi, lo, m_hi, m_lo, first, last):
                pe.matmul(acc, hi, m_hi, start=first, stop=False)
                pe.matmul(acc, hi, m_lo, start=False, stop=False)
                return pe.matmul(acc, lo, m_hi, start=False, stop=last)

            def weight(n, tile):
                s = n % SLOTS
                return w_hi[:, s, tile * P:(tile + 1) * P], w_lo[:, s, tile * P:(tile + 1) * P]

            def column_block(n, seen, acc, before=None, m_hi=xg_hi, m_lo=xg_lo):
                if seen is not None:
                    pe.wait_ge(lo_made, seen + 1)
                for k in range(KD):
                    if before is not None:
                        before(k)
                    mm = three_passes(acc, *weight(n, k), m_hi[:, k], m_lo[:, k], k == 0, k == KD - 1)
                mm.then_inc(unit_used, 1)

            def first_blocks(k):
                if k % 2 == 0:
                    pe.wait_ge(*((first_lo, k // 2 + 1) if k < 6 else (lo_made, 1)))
                pe.wait_ge(xg_made, k + 1)

            def mean_columns(stage):
                pe.wait_ge(ssq_made, KD * (stage + 1))
                for tb in range(TB):
                    mm = pe.matmul(ps_rep[:, tb:tb + 1], ssq[:, tb * P:(tb + 1) * P],
                                   scalar_of(V_MEAN_D), start=True, stop=True)
                mm.then_inc(ms_made, 1)

            def replicate(stage):
                pe.wait_ge(diag_made, stage + 1)
                pe.matmul(ps_rep, ones[:], diag, start=True, stop=True).then_inc(rep_made, 1)

            def ffn_up(base, p, stage):
                def step(f, j, first=False):
                    n = base + 2 * j
                    if not first or j >= 2:
                        pe.wait_ge(up_scaled, p * FB + f - 1)
                    if first and j == 0 and stage == 0:
                        column_block(n, None, ps[:, 0], first_blocks)
                    elif first and j == 0:
                        column_block(n, base, ps[:, 0], lambda k: pe.wait_ge(xg_made, KD * stage + k + 1))
                    else:
                        column_block(n, f * 2 + base, ps[:, 2 * (j % 2)])
                    if first and j == 1:
                        replicate(stage)
                    column_block(n + 1, f * 2 + (base + 1), ps[:, 2 * (j % 2) + 1])
                    if first and j == 0:
                        mean_columns(stage)

                step(0, 0, True)
                step(1, 1, True)
                with pe.Fori(1, FB // 2) as it:
                    step(it * 2, 2)
                    step(it * 2 + 1, 3)

            def ffn_down(base, p, out_stage):
                def step(d, j):
                    acc = ps[:, 4 + j % 2]
                    pe.wait_ge(ssq_made, d + (KD * (out_stage + 1) - 1))
                    for f in range(FB):
                        n = base + DN_UNITS * j + f // KD
                        if f == 0:
                            pe.wait_ge(act_made, p * FB + FB - 2)
                        if f == FB - 2:
                            pe.wait_ge(act_made, p * FB + FB)
                        if f % KD == 0:
                            pe.wait_ge(lo_made, d * DN_UNITS + (base + f // KD + 1))
                        mm = three_passes(acc, *weight(n, f % KD), act_hi[:, f], act_lo[:, f],
                                          f == 0, f == FB - 1)
                        if f % KD == KD - 1 or f == FB - 1:
                            mm.then_inc(unit_used, 1)

                with pe.Fori(0, KD // 4) as it:
                    for j in range(4):
                        step(it * 4 + j, j)

            def mixer():
                def spread(h):
                    bank = ps[:, r_bank[h]]
                    if h >= 1:
                        pe.wait_ge(r_copied, h)
                    if h >= 3:
                        pe.wait_ge(hm_made, h - 2)
                    for part in neg_m:
                        mm = pe.matmul(bank, sel[:, h * P:(h + 1) * P], part, start=part is neg_m[0],
                                       stop=part is neg_m[1])
                    mm.then_inc(r_rep, 1)

                def scores(h):
                    if h == 0:
                        pe.wait_ge(cols_made, 3)
                        pe.wait_ge(r_copied, 2)
                    else:
                        pe.wait_ge(p_made, h)
                    pe.wait_ge(qk_made, 2 * h + 2)
                    for S in range(TB):
                        w = T - S * P
                        keys, queries = slice(S * P, (S + 1) * P), slice(S * P, T)
                        mm = three_passes(ps_sc[:, S_OFF[S]:S_OFF[S] + w],
                                          act_hi[:, QK + 4 + h, keys], act_lo[:, QK + 4 + h, keys],
                                          act_hi[:, QK + h, queries], act_lo[:, QK + h, queries],
                                          True, True)
                    mm.then_inc(sc_made, 1)

                def values(h):
                    pe.wait_ge(p_split, h + 1)
                    if h == 0:
                        pe.wait_ge(v_made, TB)
                    else:
                        pe.wait_ge(t1_made, h)
                    for S in range(TB):
                        w = T - S * P
                        v = slice(h * P, (h + 1) * P)
                        at = slice(S_OFF[S], S_OFF[S] + w)
                        mm = three_passes(ps_num[:, S * P:T], act_hi[:, VB + S, v], act_lo[:, VB + S, v],
                                          p_hi[:, at], p_lo[:, at], S == 0, S == TB - 1)
                    for tb in range(TB):
                        for S in range(tb + 1):
                            at = S_OFF[S] + (tb - S) * P
                            for part in (p_hi, p_lo):
                                mm = pe.matmul(ps_col[:, 2 * tb:2 * tb + 2], part[:, at:at + P], ones_r[:, :],
                                               start=(S == 0 and part is p_hi), stop=(S == tb and part is p_lo))
                    mm.then_inc(num_made, 1)

                def head_mean(h):
                    pe.wait_ge(sqn_made, h + 1)
                    pe.wait_ge(hcol_step, HSTEPS * h + 1)
                    for tb in range(TB):
                        mm = pe.matmul(ps_col[:, 8 + tb:9 + tb], sqn[:, tb * P:(tb + 1) * P],
                                       scalar_of(V_MEAN_H), start=True, stop=True)
                    mm.then_inc(ms_h, 1)

                def head_rep(h):
                    pe.wait_ge(hdiag_made, h + 1)
                    pe.wait_ge(r_copied, min(h + 3, HEADS))
                    pe.matmul(ps_rep, ones[:], diag, start=True, stop=True).then_inc(h_rep, 1)

                def proj(i, mean_of=None):
                    n = O_UNIT + i
                    if i == 1:
                        pe.wait_ge(v_made, TB)
                    elif 2 <= i < HEADS + 2:
                        pe.wait_ge(o_scaled, i - 1)
                    elif i >= HEADS + 2:
                        pe.wait_ge(pu_made, i - 1 - HEADS)

                    def before(k):
                        if k == 2 and mean_of is not None:
                            head_mean(mean_of)

                    column_block(n, n, ps[:, proj_bank(i)], before)

                def pool_mix(i):
                    g = HEADS - 1 - i
                    if i == 0:
                        pe.wait_ge(pw_made, 1)
                        pe.wait_ge(p_made, HEADS)
                    if i >= 2:
                        pe.wait_ge(pmx_made, i - 1)
                    pe.wait_ge(pool_made, i + 1)
                    at = slice(g * P, (g + 1) * P)
                    three_passes(ps[:, 2 + i % 2], act_hi[:, PW, at], act_lo[:, PW, at],
                                 act_hi[:, PO + i % 2], act_lo[:, PO + i % 2], True, True).then_inc(pm_made, 1)

                column_block(MIX, MIX, ps[:, 2], lambda k: pe.wait_ge(xg_made, KD + k + 1))
                mean_columns(1)
                for i in range(2 * HEADS):
                    n = QK_UNIT + i
                    if i >= 4:
                        pe.wait_ge(u_made, i - 3)
                    column_block(n, n, ps[:, qk_bank[i % 4]])
                    if i == 0:
                        replicate(1)
                    if i == 5:
                        pe.wait_ge(cm_made, 1)
                        spread(0)
                spread(1)
                for what in range(2):
                    rows = arena[0:HEADS, 1 if what == 0 else 3]
                    for tb in range(TB):
                        at = 4 * (4 * what + tb)
                        mm = pe.matmul(ps[:, 3, at:at + 4], rows[:, tb * P:(tb + 1) * P],
                                       ident[0:HEADS, 0:HEADS], start=True, stop=True)
                mm.then_inc(cols_made, 1)
                pe.wait_ge(u_made, 6)
                for i in range(4):
                    n = V_UNIT + i
                    pe.wait_ge(lo_made, n + 1)
                    for kk in range(2):
                        k = 2 * i + kk
                        wh = w_hi[:, n % SLOTS, kk * T:(kk + 1) * T]
                        wl = w_lo[:, n % SLOTS, kk * T:(kk + 1) * T]
                        for tb in range(TB):
                            xh = xg_hi[:, k, tb * P:(tb + 1) * P]
                            xl = xg_lo[:, k, tb * P:(tb + 1) * P]
                            mm = three_passes(ps[:, v_bank[tb]], xh, xl, wh, wl, k == 0, k == KD - 1)
                    mm.then_inc(unit_used, 1)
                    if i == 0:
                        pe.wait_ge(u_made, 8)
                        scores(0)
                for h in range(HEADS):
                    proj(h, h - 1 if h else None)
                    if h + 1 < HEADS:
                        scores(h + 1)
                    if h:
                        head_rep(h - 1)
                    values(h)
                    if h + 2 < HEADS:
                        spread(h + 2)
                proj(4, HEADS - 1)
                head_rep(HEADS - 1)
                proj(5)
                proj(6)
                pool_mix(0)
                proj(7)
                pool_mix(1)

                def part(d, ks, first=False, last=False):
                    for k in ks:
                        if k >= HEADS:
                            pe.wait_ge(pmx_made, 2 * HEADS - k)
                        mm = three_passes(ps[:, 4 + d], *weight(WO_UNIT + d, k), act_hi[:, QK + k], act_lo[:, QK + k],
                                          first and k == ks[0], last and k == ks[-1])
                    if last:
                        mm.then_inc(unit_used, 1)

                pe.wait_ge(mix_made, HEADS)
                pe.wait_ge(lo_made, WO_UNIT + 1)
                part(0, (0, 1, 2, 3), first=True)
                pool_mix(2)
                part(0, (7, 6))
                pe.wait_ge(lo_made, WO_UNIT + 2)
                part(1, (0, 1, 2, 3, 7, 6), first=True)
                pool_mix(3)
                part(0, (5,))
                part(1, (5,))
                part(0, (4,), last=True)
                part(1, (4,), last=True)
                for d in range(2, KD):
                    n = WO_UNIT + d
                    pe.wait_ge(x_new, KD + d - 1)
                    column_block(n, n, ps[:, 4 + d % 2],
                                 m_hi=act_hi[:, QK:QK + KD], m_lo=act_lo[:, QK:QK + KD])

            pe.wait_ge(ones_made, 1)
            for _ in range(WARMUPS):
                pe.matmul(ps_rep, diag[:, 0:P], diag, start=True, stop=True)
            pe.wait_ge(vec_in, 16)
            pe.wait_ge(const_in, 16 * 3)
            ffn_up(UP1, 0, 0)
            ffn_down(DN1, 0, 0)
            mixer()
            ffn_up(UP2, 1, 2)
            ffn_down(DN2, 1, 2)
            mean_columns(3)
            replicate(3)

        @block.scalar
        def _(act):
            act.dma_start(vec[:], vecs).then_inc(vec_in, 16)
            for d in range(KD):
                act.dma_start(x[:, d], x_t[d * P:(d + 1) * P]).then_inc(x_in[d], 16)
            for i, t in enumerate((ident, ones, mask)):
                act.dma_start(t[:], consts[i]).then_inc(const_in, 16)
            act.dma_start(arena[:, 4], pool_w).then_inc(pw_in, 16)

            def split_hi(k, seen, loads, first=False):
                act.wait_ge(raw_in[k % RAWS], loads * 16)
                if not first:
                    act.wait_ge(unit_used, seen - (SLOTS - 1))
                act.activation(w_hi[:, k % SLOTS], raw[:, k % RAWS], ACT.Copy).then_inc(hi_made, 1)

            def prep_x(d, stage):
                if stage == 0:
                    act.wait_ge(x_in[d], 16)
                else:
                    act.wait_ge(x_new, KD * (stage - 1) + d + 1)
                if stage < 3:
                    act.activation(xg_hi[:, d], x[:, d], ACT.Copy, scale=scalar_of(V_GAIN + stage * KD + d)
                                   ).then_inc(xhi_made, 1)

            def square_x(d, stage):
                n = KD * stage + d
                if n >= 2:
                    act.wait_ge(ssq_made, n - 1)
                act.activation(sq[n % 2], x[:, d], ACT.Square).then_inc(sq_made, 1)

            def ffn_up(base, p):
                def step(f, j):
                    n = base + 2 * j
                    split_hi(n + SLOTS, f * 2 + (base + SLOTS), f + ((base + SLOTS) // 2 + 1))
                    act.wait_ge(gate_scaled, f + (p * FB + 1))
                    act.activation(gs[j % 2], gs[j % 2], ACT.Silu).then_inc(silu_made, 1)
                    split_hi(n + SLOTS + 1, f * 2 + (base + SLOTS + 1), f + ((base + SLOTS + 1) // 2 + 1))

                step(0, 0)
                step(1, 1)
                with act.Fori(1, FB // 2) as it:
                    step(it * 2, 2)
                    step(it * 2 + 1, 3)

            def out_blocks(base, per, stage):
                for d in range(KD):
                    for i in range(per):
                        n = base + per * d + SLOTS + i
                        if n < N_UNITS:
                            split_hi(n, n, n // RAWS + 1)
                    prep_x(d, stage)
                    square_x(d, stage)

            def mixer():
                nxt = [MIX + SLOTS]

                def split_next():
                    split_hi(nxt[0], nxt[0], nxt[0] // RAWS + 1)
                    nxt[0] += 1

                split_next()
                act.preload_act_table_set("natural_log_exp_and_others")
                fr = slice(32, 32 + HEADS)
                act.wait_ge(g_dve, 1)
                act.activation(arena[fr, 1], arena[fr, 0], ACT.Abs, bias=vec[fr, V_BG:V_BG + 1]).then_inc(g_act, 1)
                act.wait_ge(g_act, 1)
                act.activation(arena[fr, 1], arena[fr, 1], ACT.Exp, scale=-1.0).then_inc(g_act, 1)
                act.wait_ge(g_act, 2)
                act.activation(arena[fr, 1], arena[fr, 1], ACT.Ln, bias=ones[fr, 0:1]).then_inc(g_act, 1)
                def finish_qk(i):
                    h, is_k = i // 2, i % 2
                    act.wait_ge(conv_done, i + 1)
                    act.activation(work[:, 2 + i % 2], work[:, 2 + i % 2], ACT.Silu).then_inc(qk_silu, 1)
                    act.wait_ge(qk_silu, i + 1)
                    act.activation(act_hi[:, QK + h + HEADS * is_k], work[:, 2 + i % 2], ACT.Copy,
                                   scale=K_SCALE if is_k else 1.0).then_inc(qk_hi_made, 1)

                def copy_r(h):
                    act.wait_ge(r_rep, h + 1)
                    if h >= 2:
                        act.wait_ge(r_diag_made, h - 1)
                    act.activation(r_all[h % 2], ps[:, r_bank[h]], ACT.Copy).then_inc(r_copied, 1)

                for i in range(2 * HEADS):
                    act.wait_ge(u_made, i + 1)
                    if i >= 2:
                        act.wait_ge(qk_made, i - 1)
                    b = i // 2 + HEADS * (i % 2)
                    act.activation(work[:, 2 + i % 2], work[:, i % 2], ACT.Identity,
                                   bias=scalar_of(V_CONVB + b), scale=scalar_of(V_CONVW + 4 * b + 3)
                                   ).then_inc(conv0, 1)
                    split_next()
                    if i:
                        finish_qk(i - 1)
                    if i == 6:
                        copy_r(0)
                finish_qk(2 * HEADS - 1)
                act.wait_ge(qk_made, 2 * HEADS)
                copy_r(1)
                act.wait_ge(pw_in, 16)
                act.activation(act_hi[:, PW], arena[:, 4], ACT.Copy).then_inc(pw_hi_made, 1)
                act.wait_ge(cols_made, 1)
                act.activation(emcol[:], ps[:, 3, 16:32], ACT.Exp, scale=-1.0).then_inc(cols_made, 1)

                def gate(h):
                    act.wait_ge(o_scaled, h + 1)
                    act.activation(gate_of[h % 2], gate_of[h % 2], ACT.Sigmoid).then_inc(o_made, 1)

                def weights_of(h):
                    act.wait_ge(r_copied, h + 1)
                    if h == 0:
                        act.wait_ge(cols_made, 4)
                    else:
                        act.wait_ge(p_split, h)
                    for S in range(TB - 1):
                        act.activation(probs[:, S_OFF[S] + P:S_OFF[S] + T - S * P],
                                       r_all[h % 2][:, (S + 1) * P:T], ACT.Exp,
                                       bias=ccol[:, 4 * S + h:4 * S + h + 1])
                    act.wait_ge(r_diag_made, h + 1)
                    for S in range(TB):
                        ins = act.activation(probs[:, S_OFF[S]:S_OFF[S] + P], r_diag[:, S * P:(S + 1) * P],
                                             ACT.Exp, bias=ccol[:, 4 * S + h:4 * S + h + 1])
                    ins.then_inc(e_made, 1)

                def probs_hi(h):
                    act.wait_ge(p_made, h + 1)
                    if h >= 1:
                        act.wait_ge(num_made, h)
                    act.activation(p_hi, probs, ACT.Copy).then_inc(p_hi_made, 1)

                def square_num(h):
                    act.wait_ge(num_made, h + 1)
                    if h >= 1:
                        act.wait_ge(h_rep, h)
                    act.activation(sqn, ps_num, ACT.Square).then_inc(sqn_made, 1)

                def mixed_hi(h):
                    act.wait_ge(hm_made, h + 1)
                    act.activation(act_hi[:, QK + h], t1, ACT.Copy).then_inc(mix_hi_made, 1)

                def pool_hi(i):
                    act.wait_ge(pool_done, i + 1)
                    if i >= 2:
                        act.wait_ge(pm_made, i - 1)
                    act.activation(act_hi[:, PO + i % 2], pool_sums[i % 2][(HEADS - i) % 2], ACT.Copy).then_inc(pool_hi_made, 1)

                def pool_mixed_hi(i):
                    g = HEADS - 1 - i
                    act.wait_ge(pm_made, i + 1)
                    act.activation(act_hi[:, QK + HEADS + g], ps[:, 2 + i % 2], ACT.Copy,
                                   scale=scalar_of(V_PSC + g)).then_inc(pmx_hi, 1)

                weights_of(0)
                split_next()
                probs_hi(0)
                weights_of(1)
                split_next()
                split_next()
                for tb in range(TB):
                    act.wait_ge(unit_used, V_UNIT + 4)
                    act.activation(act_hi[:, VB + tb], ps[:, v_bank[tb]], ACT.Copy, scale=rcol[:, tb:tb + 1]
                                   ).then_inc(v_hi_made, 1)
                split_next()
                for h in range(HEADS):
                    if h:
                        square_num(h - 1)
                        if h + 1 < HEADS:
                            copy_r(h + 1)
                        probs_hi(h)
                        if h + 1 < HEADS:
                            weights_of(h + 1)
                    gate(h)
                    split_next()
                    if h:
                        mixed_hi(h - 1)
                square_num(HEADS - 1)
                split_next()
                mixed_hi(HEADS - 1)
                split_next()
                pool_hi(0)
                split_next()
                pool_hi(1)
                pool_mixed_hi(0)
                split_next()
                pool_mixed_hi(1)
                pool_hi(2)
                pool_hi(3)
                pool_mixed_hi(2)
                pool_mixed_hi(3)
                assert nxt[0] == WO_UNIT + SLOTS

            for i in range(4):
                part = slice(2 * P * i, 2 * P * (i + 1))
                act.wait_ge(first_in[i] if i < 3 else raw_in[0], 16)
                act.activation(w_hi[:, 0, part], raw[:, 0, part], ACT.Copy).then_inc(first_hi if i < 3 else hi_made, 1)
                if i == 0:
                    act.wait_ge(vec_in, 16)
                prep_x(i, 0)
            for d in range(4, KD):
                if d == 6:
                    split_hi(1, 1, 1, True)
                prep_x(d, 0)
            square_x(0, 0)
            square_x(1, 0)
            split_hi(2, 2, 2, True)
            for d in range(2, KD):
                square_x(d, 0)
            split_hi(3, 3, 2, True)
            ffn_up(UP1, 0)
            out_blocks(DN1, DN_UNITS, 1)
            mixer()
            out_blocks(WO_UNIT, 1, 2)
            ffn_up(UP2, 1)
            out_blocks(DN2, DN_UNITS, 3)

        @block.gpsimd
        def _(pool):
            pool.wait_ge(const_in, 16 * 3)
            for h in range(HEADS):
                pool.wait_ge(r_copied, h + 1)
                if h == 0:
                    pool.wait_ge(cols_made, 1)
                else:
                    pool.wait_ge(e_made, h)
                for S in range(TB):
                    at = slice(S * P, (S + 1) * P)
                    ins = pool.tensor_tensor(r_diag[:, at], r_all[h % 2][:, at], mask[:], ALU.add)
                ins.then_inc(r_diag_made, 1)

            win = 0
            for i in range(HEADS):
                g = HEADS - 1 - i
                pool.wait_ge(pu_made, i + 1)
                src = pool_u[i % 2]
                for s in range(g + 1):
                    dst = pool_sums[i % 2][s % 2]
                    sh = 1 << s
                    if s > 0:
                        pool.wait_ge(win_step, win)
                    pool.tensor_copy(dst[:, 0:sh], src[:, 0:sh])
                    pool.tensor_tensor(dst[:, sh:T], src[:, sh:T], src[:, 0:T - sh], ALU.add).then_inc(win_step, 1)
                    win += 1
                    src = dst

        @block.vector
        def _(dve):
            def split_lo(k, seen):
                dve.wait_ge(hi_made, seen + 1)
                dve.tensor_tensor(w_lo[:, k % SLOTS], raw[:, k % RAWS], f32(w_hi[:, k % SLOTS]),
                                  ALU.subtract).then_inc(lo_made, 1)

            def split_xg(d, stage):
                dve.wait_ge(xhi_made, KD * stage + d + 1)
                dve.scalar_tensor_tensor(xg_lo[:, d], x[:, d], scalar_of(V_GAIN + stage * KD + d),
                                         f32(xg_hi[:, d]), ALU.mult, ALU.subtract).then_inc(xg_made, 1)

            def add_square(d, stage):
                n = KD * stage + d
                dve.wait_ge(sq_made, n + 1)
                if d == 0:
                    dve.wait_ge(ssq_zero, stage + 1)
                else:
                    dve.wait_ge(ssq_made, n)
                dve.tensor_tensor(ssq, ssq, sq[n % 2], ALU.add).then_inc(ssq_made, 1)

            def clear_squares(stage):
                if stage:
                    dve.wait_ge(ms_made, stage)
                dve.memset(ssq, 0.0).then_inc(ssq_zero, 1)

            def rsqrt(step, count):
                def then(ins):
                    nonlocal count
                    ins.then_inc(step, 1)
                    count += 1
                    dve.wait_ge(step, count)

                then(dve.tensor_scalar(ycol[:].bitcast(I32), acol[:].bitcast(I32), 1, None, ALU.logical_shift_right))
                then(dve.tensor_scalar(ycol[:].bitcast(I32), ycol[:].bitcast(I32), -1.0, RSQRT_SEED, ALU.mult, ALU.add))
                for _ in range(3):
                    then(dve.scalar_tensor_tensor(tcol[:], ycol[:], -0.5, acol[:], ALU.mult, ALU.mult))
                    then(dve.tensor_tensor(tcol[:], tcol[:], ycol[:], ALU.mult))
                    then(dve.scalar_tensor_tensor(ycol[:], tcol[:], 1.5, ycol[:], ALU.add, ALU.mult))
                return count

            def make_diag(signal):
                for tb in range(TB):
                    ins = dve.tensor_scalar(diag[:, tb * P:(tb + 1) * P], ident[:], ycol[:, tb:tb + 1], None, ALU.mult)
                ins.then_inc(signal, 1)

            def inverse_rms(stage):
                base = STEPS * stage
                dve.wait_ge(ms_made, stage + 1)
                dve.tensor_scalar(acol[:], ps_rep[:, 0:TB], EPS, None, ALU.add).then_inc(col_step, 1)
                dve.wait_ge(col_step, base + 1)
                done = rsqrt(col_step, base + 1)
                assert done == base + STEPS
                if stage == 1:
                    dve.tensor_copy(rcol[:], ycol[:])
                make_diag(diag_made)

            def take_rinv(stage):
                dve.wait_ge(rep_made, stage + 1)
                dve.tensor_copy(rinv[:], ps_rep).then_inc(rinv_made, 1)
                dve.wait_ge(rinv_made, stage + 1)

            def ffn_up(base, p):
                def step(f, j):
                    n = base + 2 * j
                    g, u = gs[j % 2], us[j % 2]
                    G, U = ps[:, 2 * (j % 2)], ps[:, 2 * (j % 2) + 1]
                    dve.wait_ge(unit_used, f * 2 + (base + 2))
                    dve.tensor_tensor(g, G, rinv[:], ALU.mult).then_inc(gate_scaled, 1)
                    dve.tensor_tensor(u, U, rinv[:], ALU.mult).then_inc(up_scaled, 1)
                    split_lo(n + SLOTS, f * 2 + (base + SLOTS))
                    dve.wait_ge(silu_made, f + (p * FB + 1))
                    dve.wait_ge(up_scaled, f + (p * FB + 1))
                    dve.tensor_tensor(u, u, g, ALU.mult).then_inc(prod_made, 1)
                    split_lo(n + SLOTS + 1, f * 2 + (base + SLOTS + 1))
                    hi = act_hi[:, bass.ds(f, 1)].rearrange("p a n -> p (a n)")
                    lo = act_lo[:, bass.ds(f, 1)].rearrange("p a n -> p (a n)")
                    dve.wait_ge(prod_made, f + (p * FB + 1))
                    dve.tensor_scalar(hi, u, 1.0, None, ALU.mult).then_inc(act_hi_made, 1)
                    dve.wait_ge(act_hi_made, f + (p * FB + 1))
                    dve.tensor_tensor(lo, u, f32(hi), ALU.subtract).then_inc(act_made, 1)

                step(0, 0)
                step(1, 1)
                with dve.Fori(1, FB // 2) as it:
                    step(it * 2, 2)
                    step(it * 2 + 1, 3)

            def out_blocks(base, per, stage, factor):
                for d in range(KD):
                    n = base + per * d
                    for i in range(per - 1):
                        if n + SLOTS + i < N_UNITS:
                            split_lo(n + SLOTS + i, n + SLOTS + i)
                    dve.wait_ge(unit_used, n + per)
                    dve.scalar_tensor_tensor(x[:, d], ps[:, 4 + d % 2], factor, x[:, d],
                                             ALU.mult, ALU.add).then_inc(x_new, 1)
                    if n + SLOTS + per - 1 < N_UNITS:
                        split_lo(n + SLOTS + per - 1, n + SLOTS + per - 1)
                    if stage < 3:
                        dve.wait_ge(x_new, KD * (stage - 1) + d + 1)
                        split_xg(d, stage)
                    add_square(d, stage)

            def mixer():
                nxt = [MIX + SLOTS]

                def split_next():
                    split_lo(nxt[0], nxt[0])
                    nxt[0] += 1

                inverse_rms(1)
                take_rinv(1)
                R = slice(0, HEADS)
                fr = slice(32, 32 + HEADS)
                gsc, lf = arena[:, 0], arena[:, 2]

                def gates_in():
                    dve.tensor_tensor(arena[0:36, 0], ps[0:36, 2], rinv[0:36, :], ALU.mult).then_inc(g_dve, 1)
                    dve.wait_ge(g_dve, 1)
                    dve.tensor_scalar(lf[fr], gsc[fr], vec[fr, V_BG:V_BG + 1], 0.0, ALU.add, ALU.min).then_inc(g_dve, 1)
                    dve.tensor_scalar(gsc[R], gsc[R], vec[R, V_BG:V_BG + 1], None, ALU.add).then_inc(g_dve, 1)

                def gates():
                    count = [3]

                    def then(ins):
                        count[0] += 1
                        ins.then_inc(g_dve, 1)
                        dve.wait_ge(g_dve, count[0])

                    dve.wait_ge(g_dve, 3)
                    dve.wait_ge(g_act, 3)
                    then(dve.tensor_tensor(lf[fr], lf[fr], arena[fr, 1], ALU.subtract))
                    then(dve.tensor_copy(lf[R], lf[fr]))
                    B, M, m = arena[R, 1], arena[R, 5], arena[R, 3]
                    then(dve.tensor_tensor_scan(B, lf[R], lf[R], 0.0, ALU.add, ALU.min))
                    then(dve.tensor_tensor(B, gsc[R], B, ALU.subtract))
                    then(dve.tensor_tensor_scan(M, B, B, 0.0, ALU.max, ALU.max))
                    then(dve.tensor_scalar(neg_m[0], M, -1.0, None, ALU.mult))
                    dve.scalar_tensor_tensor(neg_m[1], M, -1.0, f32(neg_m[0]), ALU.mult, ALU.subtract)
                    for h in range(HEADS):
                        dve.tensor_scalar(sel[:, h * P:(h + 1) * P], ones[R, :], ident[R, h:h + 1], None, ALU.mult)
                    dve.tensor_tensor_scan(m, lf[R], gsc[R], 0.0, ALU.add, ALU.max).then_inc(cm_made, 1)

                def taps(i):
                    b = i // 2 + HEADS * (i % 2)
                    u, a = work[:, i % 2], work[:, 2 + i % 2]
                    dve.wait_ge(u_made, i + 1)
                    dve.wait_ge(conv0, i + 1)
                    for back in range(1, 4):
                        ins = dve.scalar_tensor_tensor(a[:, back:T], u[:, 0:T - back],
                                                       scalar_of(V_CONVW + 4 * b + 3 - back), a[:, back:T],
                                                       ALU.mult, ALU.add)
                        if back < 3:
                            ins.then_inc(conv_step, 1)
                            dve.wait_ge(conv_step, 2 * i + back)
                    ins.then_inc(conv_done, 1)

                def qk_lo(i):
                    b = i // 2 + HEADS * (i % 2)
                    dve.wait_ge(qk_hi_made, i + 1)
                    dve.scalar_tensor_tensor(act_lo[:, QK + b], work[:, 2 + i % 2], K_SCALE if i % 2 else 1.0,
                                             f32(act_hi[:, QK + b]), ALU.mult, ALU.subtract).then_inc(qk_made, 1)

                gates_in()
                split_next()
                for i in range(2 * HEADS):
                    dve.wait_ge(unit_used, QK_UNIT + i + 1)
                    dve.tensor_tensor(work[:, i % 2], ps[:, qk_bank[i % 4]], rinv[:], ALU.mult).then_inc(u_made, 1)
                    if i:
                        taps(i - 1)
                    split_next()
                    if i:
                        qk_lo(i - 1)
                    if i == 2:
                        gates()
                taps(2 * HEADS - 1)
                qk_lo(2 * HEADS - 1)
                dve.wait_ge(pw_hi_made, 1)
                dve.tensor_tensor(act_lo[:, PW], arena[:, 4], f32(act_hi[:, PW]), ALU.subtract).then_inc(pw_made, 1)
                dve.wait_ge(cols_made, 2)
                dve.tensor_copy(ccol[:], ps[:, 3, 0:16]).then_inc(cols_made, 1)
                dve.scalar_tensor_tensor(em2[:], emcol[:], EPS, emcol[:], ALU.mult, ALU.mult).then_inc(cols_made, 1)

                def gate(h):
                    dve.wait_ge(unit_used, O_UNIT + h + 1)
                    dve.tensor_tensor(gate_of[h % 2], ps[:, proj_bank(h)], rinv[:], ALU.mult).then_inc(o_scaled, 1)

                def probs_of(h):
                    dve.wait_ge(sc_made, h + 1)
                    dve.wait_ge(e_made, h + 1)
                    dve.tensor_tensor(probs, probs, ps_sc, ALU.mult).then_inc(p_made, 1)

                def probs_lo(h):
                    dve.wait_ge(p_made, h + 1)
                    dve.wait_ge(p_hi_made, h + 1)
                    dve.tensor_tensor(p_lo, probs, f32(p_hi), ALU.subtract).then_inc(p_split, 1)

                def head_scale(h):
                    dve.wait_ge(num_made, h + 1)
                    count = HSTEPS * h

                    def then(ins):
                        nonlocal count
                        ins.then_inc(hcol_step, 1)
                        count += 1
                        dve.wait_ge(hcol_step, count)

                    then(dve.tensor_copy(qcol[:], ps_col[:, 0:8:2]))
                    then(dve.scalar_tensor_tensor(dcol[:], qcol[:], EPS, qcol[:], ALU.mult, ALU.mult))
                    if h == 0:
                        dve.wait_ge(cols_made, 4)
                    then(dve.tensor_tensor(dcol[:], dcol[:], em2[:, h:16:4], ALU.max))
                    dve.wait_ge(sqn_made, h + 1)
                    dve.wait_ge(o_made, h + 1)
                    if h >= 1:
                        dve.wait_ge(mix_made, h)
                    dve.scalar_tensor_tensor(t1, ps_num, scalar_of(V_MH + h), gate_of[h % 2],
                                             ALU.mult, ALU.mult).then_inc(t1_made, 1)

                def head_rsqrt(h):
                    count = HSTEPS * h + 3
                    dve.wait_ge(ms_h, h + 1)
                    dve.scalar_tensor_tensor(acol[:], ps_col[:, 8:8 + TB], TINY, dcol[:],
                                             ALU.add, ALU.add).then_inc(hcol_step, 1)
                    dve.wait_ge(hcol_step, count + 1)
                    rsqrt(hcol_step, count + 1)
                    make_diag(hdiag_made)

                def mixed(h):
                    dve.wait_ge(h_rep, h + 1)
                    dve.tensor_tensor(t1, t1, ps_rep, ALU.mult).then_inc(hm_made, 1)

                def mixed_lo(h):
                    dve.wait_ge(hm_made, h + 1)
                    dve.wait_ge(mix_hi_made, h + 1)
                    dve.tensor_tensor(act_lo[:, QK + h], t1, f32(act_hi[:, QK + h]),
                                      ALU.subtract).then_inc(mix_made, 1)

                def pool_in(i):
                    dve.wait_ge(unit_used, PL_UNIT + i + 1)
                    dve.tensor_tensor(pool_u[i % 2], ps[:, proj_bank(HEADS + i)], rinv[:], ALU.mult).then_inc(pu_made, 1)

                def pool_mean(i):
                    g = HEADS - 1 - i
                    u, s, dst = pool_u[i % 2], pool_sums[i % 2][g % 2], pool_sums[i % 2][(g + 1) % 2]
                    dve.wait_ge(win_step, sum(HEADS - k for k in range(i + 1)))
                    dve.wait_ge(pu_made, i + 1)
                    inv = vec[:, V_INV + MAXWIN * g:V_INV + MAXWIN * (g + 1)]
                    dve.tensor_tensor(dst[:, 0:MAXWIN], s[:, 0:MAXWIN], inv, ALU.mult).then_inc(pool_step, 1)
                    dve.scalar_tensor_tensor(dst[:, MAXWIN:T], s[:, MAXWIN:T], 1.0 / WINDOWS[g], u[:, MAXWIN:T],
                                             ALU.mult, ALU.subtract)
                    dve.wait_ge(pool_step, i + 1)
                    dve.tensor_tensor(dst[:, 0:MAXWIN], dst[:, 0:MAXWIN], u[:, 0:MAXWIN],
                                      ALU.subtract).then_inc(pool_done, 1)

                def pool_lo(i):
                    dve.wait_ge(pool_done, i + 1)
                    dve.wait_ge(pool_hi_made, i + 1)
                    dve.tensor_tensor(act_lo[:, PO + i % 2], pool_sums[i % 2][(HEADS - i) % 2],
                                      f32(act_hi[:, PO + i % 2]), ALU.subtract).then_inc(pool_made, 1)

                def pool_mixed_lo(i):
                    g = HEADS - 1 - i
                    dve.wait_ge(pmx_hi, i + 1)
                    dve.scalar_tensor_tensor(act_lo[:, QK + HEADS + g], ps[:, 2 + i % 2], scalar_of(V_PSC + g),
                                             f32(act_hi[:, QK + HEADS + g]), ALU.mult, ALU.subtract
                                             ).then_inc(pmx_made, 1)

                split_next()
                probs_of(0)
                probs_lo(0)
                split_next()
                split_next()
                for tb in range(TB):
                    dve.wait_ge(v_hi_made, tb + 1)
                    dve.scalar_tensor_tensor(act_lo[:, VB + tb], ps[:, v_bank[tb]], rcol[:, tb:tb + 1],
                                             f32(act_hi[:, VB + tb]), ALU.mult, ALU.subtract).then_inc(v_made, 1)
                split_next()
                for h in range(HEADS):
                    if h:
                        head_scale(h - 1)
                        probs_lo(h)
                        head_rsqrt(h - 1)
                    gate(h)
                    split_next()
                    if h + 1 < HEADS:
                        probs_of(h + 1)
                    if h:
                        mixed(h - 1)
                        mixed_lo(h - 1)
                head_scale(HEADS - 1)
                head_rsqrt(HEADS - 1)
                pool_in(0)
                split_next()
                mixed(HEADS - 1)
                mixed_lo(HEADS - 1)
                pool_in(1)
                split_next()
                pool_mean(0)
                pool_lo(0)
                pool_in(2)
                split_next()
                pool_mean(1)
                pool_lo(1)
                pool_mixed_lo(0)
                pool_in(3)
                split_next()
                pool_mixed_lo(1)
                pool_mean(2)
                pool_lo(2)
                pool_mean(3)
                pool_lo(3)
                pool_mixed_lo(2)
                pool_mixed_lo(3)
                clear_squares(2)
                assert nxt[0] == WO_UNIT + SLOTS

            dve.memset(diag, 0.0).then_inc(ones_made, 1)
            dve.memset(f32(ones_r[:]), 1.0)
            clear_squares(0)
            for i in range(4):
                part = slice(2 * P * i, 2 * P * (i + 1))
                dve.wait_ge(*((first_hi, i + 1) if i < 3 else (hi_made, 1)))
                dve.tensor_tensor(w_lo[:, 0, part], raw[:, 0, part], f32(w_hi[:, 0, part]),
                                  ALU.subtract).then_inc(first_lo if i < 3 else lo_made, 1)
                if i == 0:
                    dve.wait_ge(vec_in, 16)
                split_xg(i, 0)
            for d in range(4, KD):
                split_xg(d, 0)
                if d == 6:
                    split_lo(1, 1)
            dve.wait_ge(const_in, 16 * 3)
            add_square(0, 0)
            add_square(1, 0)
            split_lo(2, 2)
            for d in range(2, KD):
                add_square(d, 0)
            split_lo(3, 3)
            inverse_rms(0)
            take_rinv(0)
            clear_squares(1)
            ffn_up(UP1, 0)
            out_blocks(DN1, DN_UNITS, 1, 0.5)
            mixer()
            out_blocks(WO_UNIT, 1, 2, 1.0)
            inverse_rms(2)
            take_rinv(2)
            clear_squares(3)
            ffn_up(UP2, 1)
            out_blocks(DN2, DN_UNITS, 3, 0.5)
            inverse_rms(3)
            dve.wait_ge(rep_made, 4)
            for d in range(KD):
                dve.scalar_tensor_tensor(x[:, d], x[:, d], scalar_of(V_GAIN + 3 * KD + d), ps_rep,
                                         ALU.mult, ALU.mult).then_inc(y_made, 1)


def _blocks(w):
    rows, cols = w.shape
    return w.reshape(rows // P, P, cols // P, P).transpose(2, 1, 0, 3).reshape(cols // P, P, rows)


def kernel(**inputs):
    import concourse.bacc as bacc
    from concourse.bass_utils import run_bass_kernel_spmd

    a = {k: np.asarray(v) for k, v in inputs.items()}

    def ffn(p):
        gate, up = _blocks(a[p + "_w_gate"][0]), _blocks(a[p + "_w_up"][0])
        yield np.stack([gate, up], 1).reshape(2 * FB, P, UNIT)
        down = np.zeros((KD, P, DN_UNITS, UNIT), np.float32)
        down.reshape(KD, P, DN_UNITS * UNIT)[:, :, :FF] = _blocks(a[p + "_w_down"][0])
        yield down.transpose(0, 2, 1, 3).reshape(DN_UNITS * KD, P, UNIT)

    def mixer():
        w = a["w_in"][0]
        half = D // 2
        gates = np.zeros((D, P), np.float32)
        gates[:, 0:HEADS] = w[:, 4 * half:4 * half + HEADS]
        gates[:, 32:32 + HEADS] = w[:, 4 * half + HEADS:4 * half + 2 * HEADS]
        yield _blocks(gates)
        q, k = _blocks(w[:, 0:half]), _blocks(w[:, half:2 * half])
        yield np.stack([q, k], 1).reshape(2 * HEADS, P, UNIT)
        v = w[:, 2 * half:3 * half].reshape(4, 2, P, half)
        yield v.transpose(0, 2, 1, 3).reshape(4, P, UNIT)
        yield _blocks(w[:, 3 * half:4 * half])
        yield _blocks(w[:, 4 * half + 2 * HEADS:])[::-1]
        yield _blocks(a["w_out"][0])

    weights = np.concatenate([*ffn("ffn1"), *mixer(), *ffn("ffn2")])
    pool_w = a["pool_w"][0].transpose(1, 0, 2).reshape(P, HEADS * P)

    vecs = np.zeros((P, N_VEC), np.float32)

    def columns(at, v):
        vecs[:, at:at + v.size // P] = v.reshape(-1, P).T

    for i, g in enumerate((a["ffn1_norm"][0], a["mix_norm"][0], a["ffn2_norm"][0], a["final_norm"])):
        columns(V_GAIN + KD * i, g)
    vecs[:, V_CONVW:V_CONVB] = a["conv_w"][0].reshape(4, KD, P).transpose(2, 1, 0).reshape(P, 4 * KD)
    columns(V_CONVB, a["conv_b"][0])
    columns(V_MH, a["mh_norm"][0])
    columns(V_PSC, a["pool_scale"][0])
    vecs[0:HEADS, V_BG] = a["b_gates"][0, 0:HEADS]
    vecs[32:32 + HEADS, V_BG] = a["b_gates"][0, HEADS:]
    vecs[:, V_MEAN_D], vecs[:, V_MEAN_H] = 1.0 / D, 1.0 / P
    for g, win in enumerate(WINDOWS):
        at = V_INV + MAXWIN * g
        vecs[:, at:at + MAXWIN] = (1.0 / np.minimum(np.arange(1, MAXWIN + 1), win)).astype(np.float32)
    causal = np.arange(P)[:, None] <= np.arange(P)[None, :]
    consts = np.stack([np.eye(P), np.ones((P, P)), np.where(causal, 0.0, -1e30)]).astype(np.float32)

    arrays = {"weights": weights, "pool_w": pool_w, "x_t": a["x"][0].T, "vecs": vecs, "consts": consts}
    arrays = {k: np.ascontiguousarray(v) for k, v in arrays.items()}
    nc = bacc.Bacc("TRN2", target_bir_lowering=False, num_devices=1)
    args = [nc.dram_tensor(k, v.shape, F32, kind="ExternalInput").ap() for k, v in arrays.items()]
    out = nc.dram_tensor("out", (D, T), F32, kind="ExternalOutput").ap()
    build_layer(nc, *args, out)
    r = run_bass_kernel_spmd(nc, [arrays], core_ids=[0])
    return np.ascontiguousarray(r.results[0]["out"].T).reshape(1, T, D)
```

```python
from contextlib import ExitStack

import numpy as np

import concourse.bass as bass
from concourse import mybir

F32 = mybir.dt.float32
F32R = mybir.dt.float32r
I32 = mybir.dt.int32
ALU = mybir.AluOpType
ACT = mybir.ActivationFunctionType

P = 128
T = 512
D = 1024
KD = D // P
FF = 2816
FB = FF // P
HEADS = 4
TB = T // P
EPS = 1e-6
K_SCALE = float(P) ** -0.5
WINDOWS = (2, 4, 8, 16)
MAXWIN = 16
TINY = 1e-37
RSQRT_SEED = float(0x5F3759DF)

UNIT = 8 * P
SLOTS = 4
RAWS = 2
DN_UNITS = 3
UP1 = 0
DN1 = UP1 + 2 * FB
MIX = DN1 + DN_UNITS * KD
QK_UNIT = [MIX + i for i in (1, 2, 3, 4, 6, 7, 9, 10)]
V_UNIT = [MIX + i for i in (5, 8, 11, 12)]
O_UNIT = MIX + 13
PL_UNIT = O_UNIT + HEADS
WO_UNIT = PL_UNIT + HEADS
UP2 = WO_UNIT + KD
DN2 = UP2 + 2 * FB
N_UNITS = DN2 + DN_UNITS * KD

HALF = T // 2
STORES = ((0, 2), (2, 2), (4, 2), (6, 1), (7, 1))
POOL_SQ = 4
WARMUPS = 5
SUMW = 64
STEPS = 12
HSTEPS = STEPS + 3
MEAN_AT = (4, 5, 5, 3, 4)

V_GAIN = 0
V_CONVW = V_GAIN + 4 * KD
V_CONVB = V_CONVW + 4 * KD
V_MH = V_CONVB + KD
V_PSC = V_MH + HEADS
V_BG = V_PSC + HEADS
V_MEAN_D = V_BG + 1
V_MEAN_H = V_MEAN_D + 1
V_INV = V_MEAN_H + 1
N_VEC = V_INV + HEADS * MAXWIN

S_OFF = {0: 0, 1: 512, 3: 896, 2: 1024}
S_COLS = 1280


def build_layer(nc, weights, pool_w, x_t, vecs, consts, out):
    ctx = ExitStack()
    with ctx:
        def sb(name, shape, dt=F32):
            return ctx.enter_context(nc.sbuf_tensor(name, shape, dt))

        def sem(name):
            return ctx.enter_context(nc.semaphore(name))

        raw = sb("raw", [P, RAWS, UNIT])
        w_hi = sb("w_hi", [P, SLOTS, UNIT], F32R)
        w_lo = sb("w_lo", [P, SLOTS, UNIT], F32R)
        x = sb("x", [P, KD, T])
        xg_hi = sb("xg_hi", [P, KD, T], F32R)
        xg_lo = sb("xg_lo", [P, KD, T], F32R)
        act_hi = sb("act_hi", [P, FB, T], F32R)
        act_lo = sb("act_lo", [P, FB, T], F32R)
        QK, VB, SC, PO, PW, NM, SEL = 0, 8, 12, 15, 17, 18, 19
        work = sb("work", [P, 5, T])
        arena = sb("arena", [P, 6, T])
        rinv = sb("rinv", [P, T])
        vec = sb("vec", [P, N_VEC])
        ident = sb("ident", [P, P])
        ones = sb("ones", [P, P])
        mask = sb("mask", [P, P])
        key_sum = sb("key_sum", [P, T])
        rcol = sb("rcol", [P, TB])
        ycol = sb("ycol", [P, TB])
        tcol = sb("tcol", [P, TB])
        acol = sb("acol", [P, TB])
        qcol = sb("qcol", [P, TB])
        dcol = sb("dcol", [P, TB])
        cols = sb("cols", [P, 2 * TB * HEADS])
        emcol = sb("emcol", [P, TB * HEADS])
        em2 = sb("em2", [P, TB * HEADS])

        ps = ctx.enter_context(nc.psum_tensor("ps", [P, 8, T], F32))

        ccol, mcol = cols[:, 0:TB * HEADS], cols[:, TB * HEADS:]
        gs, us = (work[:, 0], work[:, 1]), (work[:, 2], work[:, 3])
        sq, ssq = (work[:, 2], work[:, 3]), work[:, 4]
        zeros = arena[:, 5]
        probs = arena[:, 0:3].rearrange("p a n -> p (a n)")[:, 0:S_COLS]
        r_diag, t1, sqn = arena[:, 3], arena[:, 4], arena[:, 5]
        r_all = (work[:, 4], work[:, 3])
        gate_of = (work[:, 0], work[:, 1])
        pool_u = (work[:, 2], work[:, 0])
        pool_sums = ((work[:, 3], work[:, 4]), (arena[:, 0], arena[:, 1]))
        neg_m = (act_hi[0:HEADS, NM], act_lo[0:HEADS, NM])
        sel = act_hi[0:HEADS, SEL]
        p_hi = act_hi[:, SC:SC + 3].rearrange("p a n -> p (a n)")[:, 0:S_COLS]
        p_lo = act_lo[:, SC:SC + 3].rearrange("p a n -> p (a n)")[:, 0:S_COLS]
        ps_sc = ps[:, 2:5].rearrange("p a n -> p (a n)")[:, 0:S_COLS]
        ps_num, ps_col, ps_rep = ps[:, 5], ps[:, 6], ps[:, 7]
        qk_bank = (1, 4, 3)
        v_bank = (0, 7, 5, 6)
        r_bank = (2, 7, 7, 7)

        def proj_bank(i):
            return (1 + i) % 2

        raw_in = [sem(f"raw_in{i}") for i in range(RAWS)]
        x_in = [sem(f"x_in{i}") for i in range(KD)]
        first_in = [sem(f"first_in{i}") for i in range(KD - 2)]
        vec_in, const_in, pw_in, stored = sem("vec_in"), sem("const_in"), sem("pw_in"), sem("stored")
        first_hi, first_lo = sem("first_hi"), sem("first_lo")
        early_in = sem("early_in")
        hi_made, lo_made, unit_used = sem("hi_made"), sem("lo_made"), sem("unit_used")
        x_new, xhi_made, xg_made = sem("x_new"), sem("xhi_made"), sem("xg_made")
        pool_sq = sem("pool_sq")
        sq_made, ssq_made, ssq_zero = sem("sq_made"), sem("ssq_made"), sem("ssq_zero")
        ms_made, rep_made, rinv_made = sem("ms_made"), sem("rep_made"), sem("rinv_made")
        col_step = sem("col_step")
        gate_scaled, silu_made, up_scaled = sem("gate_scaled"), sem("silu_made"), sem("up_scaled")
        prod_made, act_hi_made, act_made = sem("prod_made"), sem("act_hi_made"), sem("act_made")
        u_made, conv0, conv_step, conv_done = sem("u_made"), sem("conv0"), sem("conv_step"), sem("conv_done")
        qk_silu, qk_hi_made, qk_made = sem("qk_silu"), sem("qk_hi_made"), sem("qk_made")
        g_dve, g_act, cm_made, cols_made = sem("g_dve"), sem("g_act"), sem("cm_made"), sem("cols_made")
        v_hi_made, v_made = sem("v_hi_made"), sem("v_made")
        o_scaled, o_made = sem("o_scaled"), sem("o_made")
        r_rep, r_copied, r_diag_made, e_made = sem("r_rep"), sem("r_copied"), sem("r_diag_made"), sem("e_made")
        sc_made, p_made, p_hi_made, p_split = sem("sc_made"), sem("p_made"), sem("p_hi_made"), sem("p_split")
        ks_step, ks_made = sem("ks_step"), sem("ks_made")
        num_made, sqn_made, t1_made, ms_h = sem("num_made"), sem("sqn_made"), sem("t1_made"), sem("ms_h")
        hcol_step, h_rep, hm_made = sem("hcol_step"), sem("h_rep"), sem("hm_made")
        mix_hi_made, mix_made = sem("mix_hi_made"), sem("mix_made")
        pu_made, win_step, pool_step, pool_done = sem("pu_made"), sem("win_step"), sem("pool_step"), sem("pool_done")
        pool_hi_made, pool_made, pm_made = sem("pool_hi_made"), sem("pool_made"), sem("pm_made")
        pw_hi_made, pw_made, pmx_hi, pmx_made = sem("pw_hi_made"), sem("pw_made"), sem("pmx_hi"), sem("pmx_made")
        zeros_made, y_made = sem("zeros_made"), sem("y_made")
        last_made, last_x, last_sq = sem("last_made"), sem("last_x"), sem("last_sq")
        gained, last_rinv, ya_made = sem("gained"), sem("last_rinv"), sem("ya_made")

        block = ctx.enter_context(nc.Block())

        def scalar_of(col):
            return vec[:, col:col + 1]

        def f32(ap):
            return ap.bitcast(F32)

        def first_part(i):
            return i % 2, slice(2 * P * (i // 2), 2 * P * (i // 2 + 1))

        @block.sync
        def _(sp):
            def load(n, k):
                sp.dma_start(raw[:, k % RAWS], weights[bass.ds(n, 1)].rearrange("a p n -> p (a n)")
                             ).then_inc(raw_in[k % RAWS], 16)

            sp.dma_start(vec[:], vecs).then_inc(vec_in, 16)
            for i in range(KD):
                n, part = first_part(i)
                sp.dma_start(raw[:, n, part], weights[n, :, part]).then_inc(first_in[i] if i < KD - 2 else raw_in[n], 16)
                sp.dma_start(x[:, i], x_t[i * P:(i + 1) * P]).then_inc(x_in[i], 16)
            early = slice(0, 6 * P)
            sp.wait_ge(first_lo, KD - 3)
            sp.dma_start(raw[:, 0, early], weights[2, :, early]).then_inc(early_in, 16)
            sp.wait_ge(lo_made, 1)
            sp.dma_start(raw[:, 0, 6 * P:], weights[2, :, 6 * P:]).then_inc(raw_in[0], 16)
            sp.wait_ge(lo_made, 2)
            load(3, 3)
            loops = (N_UNITS - RAWS) // RAWS
            with sp.Fori(1, loops) as it:
                for j in range(RAWS):
                    sp.wait_ge(lo_made, it * RAWS + (j + 1))
                    load(it * RAWS + (RAWS + j), RAWS + j)
            for n in range(RAWS + loops * RAWS, N_UNITS):
                sp.wait_ge(lo_made, n - RAWS + 1)
                load(n, n)
            for a, made in enumerate((ya_made, y_made)):
                at = slice(a * HALF, (a + 1) * HALF)
                for d, n in STORES:
                    sp.wait_ge(made, d + n)
                    sp.dma_start(out[d * P:(d + n) * P, at].rearrange("(n p) t -> p n t", p=P),
                                 x[:, d:d + n, at]).then_inc(stored, 16)
            sp.wait_ge(stored, 2 * 16 * len(STORES))

        @block.tensor
        def _(pe):
            def three_passes(acc, hi, lo, m_hi, m_lo, first, last):
                pe.matmul(acc, hi, m_hi, start=first, stop=False)
                pe.matmul(acc, hi, m_lo, start=False, stop=False)
                return pe.matmul(acc, lo, m_hi, start=False, stop=last)

            def weight(n, tile):
                s = n % SLOTS
                return w_hi[:, s, tile * P:(tile + 1) * P], w_lo[:, s, tile * P:(tile + 1) * P]

            def column_block(n, seen, acc, before=None, m_hi=xg_hi, m_lo=xg_lo):
                pe.wait_ge(lo_made, seen + 1)
                for k in range(KD):
                    if before is not None:
                        before(k)
                    mm = three_passes(acc, *weight(n, k), m_hi[:, k], m_lo[:, k], k == 0, k == KD - 1)
                mm.then_inc(unit_used, 1)

            def first_units():
                for k in range(KD):
                    pe.wait_ge(xg_made, k + 1)
                    for n in range(2):
                        i = 2 * (k // 2) + n
                        if k % 2 == 0:
                            pe.wait_ge(*((first_lo, i + 1) if i < KD - 2 else (lo_made, n + 1)))
                        mm = three_passes(ps[:, n], *weight(n, k), xg_hi[:, k], xg_lo[:, k], k == 0, k == KD - 1)
                        if k == KD - 1:
                            mm.then_inc(unit_used, 1)

            def spread_columns(dst, blocks):
                for tb in blocks:
                    mm = pe.matmul(dst[:, tb * P:(tb + 1) * P], ycol[:, tb:tb + 1].broadcast_to([P, P]), ident[:],
                                   start=True, stop=True)
                return mm

            def mean_columns(stage):
                pe.wait_ge(ssq_made, KD * (stage + 1))
                for tb in range(TB):
                    mm = pe.matmul(ps_rep[:, tb:tb + 1], ssq[:, tb * P:(tb + 1) * P],
                                   scalar_of(V_MEAN_D), start=True, stop=True)
                mm.then_inc(ms_made, 1)

            def replicate(stage):
                pe.wait_ge(col_step, STEPS * (stage + 1))
                spread_columns(ps_rep, range(TB)).then_inc(rep_made, 1)

            def ffn_up(base, p, stage, mean_at, rep_at):
                def step(f, j, first=False):
                    n = base + 2 * j
                    if not first or j >= 2:
                        pe.wait_ge(up_scaled, p * FB + f - 1)

                    def before(unit):
                        def hook(k):
                            if unit == 0:
                                pe.wait_ge(xg_made, KD * stage + k + 1)
                            if (unit, k) == mean_at:
                                mean_columns(stage)
                            if (unit, k) == rep_at:
                                replicate(stage)
                        return hook if first else None

                    if first and n == 0:
                        first_units()
                        return
                    for i in range(2):
                        column_block(n + i, f * 2 + (base + i), ps[:, 2 * (j % 2) + i], before(2 * j + i))

                step(0, 0, True)
                step(1, 1, True)
                with pe.Fori(1, FB // 2) as it:
                    step(it * 2, 2)
                    step(it * 2 + 1, 3)

            def down_block(base, p, out_stage, d, j):
                acc = ps[:, 4 + j % 2]
                pe.wait_ge(ssq_made, d + (KD * (out_stage + 1) - 1))
                for f in range(FB):
                    n = base + DN_UNITS * j + f // KD
                    if f == 0:
                        pe.wait_ge(act_made, p * FB + FB - 2)
                    if f == FB - 2:
                        pe.wait_ge(act_made, p * FB + FB)
                    if f % KD == 0:
                        pe.wait_ge(lo_made, d * DN_UNITS + (base + f // KD + 1))
                    mm = three_passes(acc, *weight(n, f % KD), act_hi[:, f], act_lo[:, f],
                                      f == 0, f == FB - 1)
                    if f % KD == KD - 1 or f == FB - 1:
                        mm.then_inc(unit_used, 1)

            def ffn_down(base, p, out_stage, loops):
                with pe.Fori(0, loops) as it:
                    for j in range(4):
                        down_block(base, p, out_stage, it * 4 + j, j)

            def last_blocks():
                def mean_of_half(a):
                    for tb in range(2 * a, 2 * a + 2):
                        at = slice(tb * P, (tb + 1) * P)
                        if a == 0 and tb == 0:
                            pe.wait_ge(ssq_made, 4 * KD - 1)
                        if tb == 2 * a:
                            pe.wait_ge(last_sq, a + 1)
                        pe.matmul(ps_rep[:, tb:tb + 1], ssq[:, at], scalar_of(V_MEAN_D), start=True, stop=False)
                        mm = pe.matmul(ps_rep[:, tb:tb + 1], sq[1][:, at], scalar_of(V_MEAN_D), start=False, stop=True)
                    mm.then_inc(ms_made, 1)

                def spread_half(a):
                    pe.wait_ge(col_step, STEPS * (4 + a))
                    spread_columns(ps[:, 6], range(2 * a, 2 * a + 2)).then_inc(rep_made, 1)

                for d in range(KD - 4, KD - 1):
                    down_block(DN2, 1, 2, d, d % 4)
                base = DN2 + DN_UNITS * (KD - 1)
                pe.wait_ge(ssq_made, 4 * KD - 2)
                for a in range(2):
                    at = slice(a * HALF, (a + 1) * HALF)
                    for f in range(FB):
                        n = base + f // KD
                        if a == 0 and f % KD == 0:
                            pe.wait_ge(lo_made, n + 1)
                        if a == 1 and f == 6:
                            mean_of_half(0)
                        if a == 1 and f == 19:
                            spread_half(0)
                        mm = three_passes(ps[:, 5 - 2 * a, 0:HALF], *weight(n, f % KD), act_hi[:, f, at], act_lo[:, f, at],
                                          f == 0, f == FB - 1)
                    mm.then_inc(last_made, 1)
                mean_of_half(1)
                spread_half(1)

            def mixer():
                def spread(h):
                    bank = ps[:, r_bank[h]]
                    if h == 1:
                        pe.wait_ge(v_made, 2)
                    elif h >= 2:
                        pe.wait_ge(r_copied, h)
                    if h == 3:
                        pe.wait_ge(hm_made, h - 2)
                    for part in neg_m:
                        mm = pe.matmul(bank, sel[:, h * P:(h + 1) * P], part, start=part is neg_m[0],
                                       stop=part is neg_m[1])
                    mm.then_inc(r_rep, 1)

                def scores(h):
                    if h == 0:
                        pe.wait_ge(cols_made, 2)
                        pe.wait_ge(r_copied, 1)
                        pe.wait_ge(u_made, 2 * HEADS)
                    else:
                        pe.wait_ge(p_made, h)
                    pe.wait_ge(qk_made, 2 * h + 2)
                    for S in range(TB):
                        w = T - S * P
                        keys, queries = slice(S * P, (S + 1) * P), slice(S * P, T)
                        mm = three_passes(ps_sc[:, S_OFF[S]:S_OFF[S] + w],
                                          act_hi[:, QK + 4 + h, keys], act_lo[:, QK + 4 + h, keys],
                                          act_hi[:, QK + h, queries], act_lo[:, QK + h, queries],
                                          True, True)
                    mm.then_inc(sc_made, 1)

                def values(h):
                    pe.wait_ge(p_split, h + 1)
                    if h == 0:
                        pe.wait_ge(v_made, TB)
                    else:
                        pe.wait_ge(t1_made, h)
                    for S in range(TB):
                        w = T - S * P
                        v = slice(h * P, (h + 1) * P)
                        at = slice(S_OFF[S], S_OFF[S] + w)
                        three_passes(ps_num[:, S * P:T], act_hi[:, VB + S, v], act_lo[:, VB + S, v],
                                          p_hi[:, at], p_lo[:, at], S == 0, S == TB - 1)
                        if S == 0:
                            pe.wait_ge(ks_made, h + 1)
                        mm = pe.matmul(ps_col[:, SUMW * S:SUMW * (S + 1)], key_sum[:, S * P:(S + 1) * P],
                                       ones[:, 0:SUMW], start=True, stop=True)
                    mm.then_inc(num_made, 1)

                def head_mean(h):
                    pe.wait_ge(sqn_made, h + 1)
                    pe.wait_ge(hcol_step, HSTEPS * h + 1)
                    for tb in range(TB):
                        mm = pe.matmul(ps_col[:, SUMW * TB + tb:SUMW * TB + tb + 1], sqn[:, tb * P:(tb + 1) * P],
                                       scalar_of(V_MEAN_H), start=True, stop=True)
                    mm.then_inc(ms_h, 1)

                def head_rep(h):
                    pe.wait_ge(hcol_step, HSTEPS * (h + 1))
                    pe.wait_ge(r_copied, min(h + 3, HEADS))
                    spread_columns(ps_rep, range(TB)).then_inc(h_rep, 1)

                def proj(i, mean_of=None, rep_of=None):
                    n = O_UNIT + i
                    if i == 1:
                        pe.wait_ge(v_made, 1)
                    elif 2 <= i < HEADS + 2:
                        pe.wait_ge(o_scaled, i - 1)
                    elif i >= HEADS + 2:
                        pe.wait_ge(pu_made, i - 1 - HEADS)

                    def before(k):
                        if i == 1 and k == 3:
                            values(0)
                            spread(2)
                        if mean_of is not None and k == MEAN_AT[i]:
                            head_mean(mean_of)
                        if k == 2 and rep_of is not None:
                            head_rep(rep_of)

                    column_block(n, n, ps[:, proj_bank(i)], before)

                def pool_mix(i):
                    g = HEADS - 1 - i
                    if i == 0:
                        pe.wait_ge(pw_made, 1)
                        pe.wait_ge(p_made, HEADS)
                    if i >= 2:
                        pe.wait_ge(pmx_made, i - 1)
                    pe.wait_ge(pool_made, i + 1)
                    at = slice(g * P, (g + 1) * P)
                    three_passes(ps[:, 2 + i % 2], act_hi[:, PW, at], act_lo[:, PW, at],
                                 act_hi[:, PO + i % 2], act_lo[:, PO + i % 2], True, True).then_inc(pm_made, 1)

                column_block(MIX, MIX, ps[:, 2], lambda k: pe.wait_ge(xg_made, KD + k + 1))
                mean_columns(1)
                for n in range(MIX + 1, O_UNIT):
                    if n in QK_UNIT:
                        i = QK_UNIT.index(n)
                        if i >= 3:
                            pe.wait_ge(u_made, i - 2)
                        column_block(n, n, ps[:, qk_bank[i % 3]])
                        if i == 0:
                            replicate(1)
                        continue
                    i = V_UNIT.index(n)
                    pe.wait_ge(lo_made, n + 1)
                    for kk in range(2):
                        k = 2 * i + kk
                        wh = w_hi[:, n % SLOTS, kk * T:(kk + 1) * T]
                        wl = w_lo[:, n % SLOTS, kk * T:(kk + 1) * T]
                        for tb in range(TB):
                            xh = xg_hi[:, k, tb * P:(tb + 1) * P]
                            xl = xg_lo[:, k, tb * P:(tb + 1) * P]
                            mm = three_passes(ps[:, v_bank[tb]], xh, xl, wh, wl, k == 0, k == KD - 1)
                    mm.then_inc(unit_used, 1)
                    if i == 2:
                        pe.wait_ge(cm_made, 1)
                        pe.wait_ge(u_made, 6)
                        for what in range(2):
                            rows = arena[0:HEADS, 1 if what == 0 else 3]
                            for tb in range(TB):
                                at = 4 * (4 * what + tb)
                                mm = pe.transpose(ps[:, 3, at:at + 4], rows[:, tb * P:(tb + 1) * P],
                                                  ident[0:HEADS, 0:HEADS])
                        mm.then_inc(cols_made, 1)
                        spread(0)
                scores(0)
                for h in range(HEADS):
                    proj(h, h - 1 if h else None)
                    if h + 1 < HEADS:
                        scores(h + 1)
                    if h == 0:
                        spread(1)
                    else:
                        head_rep(h - 1)
                        values(h)
                        if h + 2 < HEADS:
                            spread(h + 2)
                proj(4, HEADS - 1)
                proj(5, rep_of=HEADS - 1)
                proj(6)
                pool_mix(0)
                proj(7)
                pool_mix(1)

                def part(d, ks, first=False, last=False):
                    for k in ks:
                        if k >= HEADS:
                            pe.wait_ge(pmx_made, 2 * HEADS - k)
                        mm = three_passes(ps[:, 4 + d], *weight(WO_UNIT + d, k), act_hi[:, QK + k], act_lo[:, QK + k],
                                          first and k == ks[0], last and k == ks[-1])
                    if last:
                        mm.then_inc(unit_used, 1)

                pe.wait_ge(mix_made, HEADS)
                pe.wait_ge(lo_made, WO_UNIT + 1)
                part(0, (0, 1, 2, 3), first=True)
                pool_mix(2)
                part(0, (7, 6))
                pe.wait_ge(lo_made, WO_UNIT + 2)
                part(1, (0, 1, 2, 3, 7, 6), first=True)
                pool_mix(3)
                part(0, (5,))
                part(1, (5,))
                part(0, (4,), last=True)
                part(1, (4,), last=True)
                for d in range(2, KD):
                    n = WO_UNIT + d
                    if d >= 4:
                        pe.wait_ge(x_new, KD + d - 3)
                    column_block(n, n, ps[:, 4 + d % 4],
                                 m_hi=act_hi[:, QK:QK + KD], m_lo=act_lo[:, QK:QK + KD])

            pe.wait_ge(zeros_made, 1)
            for _ in range(WARMUPS):
                pe.matmul(ps_rep[:, 0:HALF], zeros[:, 0:P], zeros[:, 0:HALF], start=True, stop=True)
            pe.wait_ge(vec_in, 16)
            pe.wait_ge(const_in, 16 * 3)
            ffn_up(UP1, 0, 0, (2, 4), (3, 2))
            ffn_down(DN1, 0, 0, KD // 4)
            mixer()
            ffn_up(UP2, 1, 2, (1, 2), (2, 3))
            ffn_down(DN2, 1, 2, KD // 4 - 1)
            last_blocks()

        @block.scalar
        def _(act):
            act.preload_act_table_set("silu_and_others")

            def split_hi(k, seen, loads, first=False):
                act.wait_ge(raw_in[k % RAWS], loads * 16)
                if not first:
                    act.wait_ge(unit_used, seen - (SLOTS - 1))
                act.activation(w_hi[:, k % SLOTS], raw[:, k % RAWS], ACT.Copy).then_inc(hi_made, 1)

            def prep_x(d, stage):
                if stage == 0:
                    act.wait_ge(x_in[d], 16)
                else:
                    act.wait_ge(x_new, KD * (stage - 1) + d + 1)
                if stage < 3:
                    act.activation(xg_hi[:, d], x[:, d], ACT.Copy, scale=scalar_of(V_GAIN + stage * KD + d)
                                   ).then_inc(xhi_made, 1)

            def square_x(d, stage):
                n = KD * stage + d
                if n >= 2:
                    act.wait_ge(ssq_made, n - 1)
                act.activation(sq[n % 2], x[:, d], ACT.Square).then_inc(sq_made, 1)

            def ffn_up(base, p):
                def step(f, j):
                    n = base + 2 * j
                    split_hi(n + SLOTS, f * 2 + (base + SLOTS), f + ((base + SLOTS) // 2 + 1))
                    act.wait_ge(gate_scaled, f + (p * FB + 1))
                    act.activation(gs[j % 2], gs[j % 2], ACT.Silu).then_inc(silu_made, 1)
                    split_hi(n + SLOTS + 1, f * 2 + (base + SLOTS + 1), f + ((base + SLOTS + 1) // 2 + 1))

                step(0, 0)
                step(1, 1)
                with act.Fori(1, FB // 2) as it:
                    step(it * 2, 2)
                    step(it * 2 + 1, 3)

            def out_blocks(base, per, stage):
                for d in range(KD):
                    for i in range(per):
                        n = base + per * d + SLOTS + i
                        if n < N_UNITS:
                            split_hi(n, n, n // RAWS + 1)
                    if stage == 3 and d == KD - 1:
                        last_gains()
                        continue
                    prep_x(d, stage)
                    square_x(d, stage)
                    if stage == 3:
                        act.wait_ge(sq_made, KD * stage + d - POOL_SQ + 1)
                        act.activation(x[:, d], x[:, d], ACT.Copy, scale=scalar_of(V_GAIN + 3 * KD + d)
                                       ).then_inc(gained, 1)

            def last_gains():
                for a in range(2):
                    at = slice(a * HALF, (a + 1) * HALF)
                    act.wait_ge(last_sq, a + 1)
                    act.activation(x[:, KD - 1, at], x[:, KD - 1, at], ACT.Copy,
                                   scale=scalar_of(V_GAIN + 4 * KD - 1)).then_inc(gained, 1)

            def mixer():
                nxt = [MIX + SLOTS]

                def split_next():
                    split_hi(nxt[0], nxt[0], nxt[0] // RAWS + 1)
                    nxt[0] += 1

                split_next()
                act.preload_act_table_set("natural_log_exp_and_others")
                fr = slice(32, 32 + HEADS)
                act.wait_ge(g_dve, 1)
                act.activation(arena[fr, 1], arena[fr, 0], ACT.Abs, bias=vec[fr, V_BG:V_BG + 1]).then_inc(g_act, 1)
                act.wait_ge(g_act, 1)
                act.activation(arena[fr, 1], arena[fr, 1], ACT.Exp, scale=-1.0).then_inc(g_act, 1)
                act.wait_ge(g_act, 2)
                act.activation(arena[fr, 1], arena[fr, 1], ACT.Ln, bias=ones[fr, 0:1]).then_inc(g_act, 1)
                def finish_qk(i):
                    h, is_k = i // 2, i % 2
                    act.wait_ge(conv_done, i + 1)
                    act.activation(work[:, 2 + i % 2], work[:, 2 + i % 2], ACT.Silu).then_inc(qk_silu, 1)
                    act.wait_ge(qk_silu, i + 1)
                    act.activation(act_hi[:, QK + h + HEADS * is_k], work[:, 2 + i % 2], ACT.Copy,
                                   scale=K_SCALE if is_k else 1.0).then_inc(qk_hi_made, 1)

                def copy_r(h):
                    act.wait_ge(r_rep, h + 1)
                    if h >= 2:
                        act.wait_ge(r_diag_made, h - 1)
                    act.activation(r_all[h % 2], ps[:, r_bank[h]], ACT.Copy).then_inc(r_copied, 1)

                pending = None
                for n in range(MIX + 1, V_UNIT[2]):
                    if n in QK_UNIT:
                        i = QK_UNIT.index(n)
                        act.wait_ge(u_made, i + 1)
                        if i >= 2:
                            act.wait_ge(qk_made, i - 1)
                        b = i // 2 + HEADS * (i % 2)
                        act.activation(work[:, 2 + i % 2], work[:, i % 2], ACT.Identity,
                                       bias=scalar_of(V_CONVB + b), scale=scalar_of(V_CONVW + 4 * b + 3)
                                       ).then_inc(conv0, 1)
                    else:
                        finish_qk(pending)
                        pending = None
                    split_next()
                    if pending is not None:
                        finish_qk(pending)
                    pending = i if n in QK_UNIT else None
                copy_r(0)
                finish_qk(pending)
                act.wait_ge(cols_made, 2)
                act.activation(emcol[:], mcol, ACT.Exp, scale=-1.0).then_inc(cols_made, 1)

                def gate(h):
                    act.wait_ge(o_scaled, h + 1)
                    act.activation(gate_of[h % 2], gate_of[h % 2], ACT.Sigmoid).then_inc(o_made, 1)

                def weights_of(h):
                    act.wait_ge(r_copied, h + 1)
                    if h == 0:
                        act.wait_ge(cols_made, 2)
                    else:
                        act.wait_ge(p_split, h)
                        act.wait_ge(ks_made, h)
                    for S in range(TB - 1):
                        act.activation(probs[:, S_OFF[S] + P:S_OFF[S] + T - S * P],
                                       r_all[h % 2][:, (S + 1) * P:T], ACT.Exp,
                                       bias=ccol[:, 4 * S + h:4 * S + h + 1])
                    act.wait_ge(r_diag_made, h + 1)
                    for S in range(TB):
                        ins = act.activation(probs[:, S_OFF[S]:S_OFF[S] + P], r_diag[:, S * P:(S + 1) * P],
                                             ACT.Exp, bias=ccol[:, 4 * S + h:4 * S + h + 1])
                    ins.then_inc(e_made, 1)

                def probs_hi(h):
                    act.wait_ge(p_made, h + 1)
                    if h >= 1:
                        act.wait_ge(num_made, h)
                    act.activation(p_hi, probs, ACT.Copy).then_inc(p_hi_made, 1)

                def square_num(h):
                    act.wait_ge(num_made, h + 1)
                    if h >= 1:
                        act.wait_ge(ms_h, h)
                    act.activation(sqn, ps_num, ACT.Square).then_inc(sqn_made, 1)

                def mixed_hi(h):
                    act.wait_ge(hm_made, h + 1)
                    act.activation(act_hi[:, QK + h], t1, ACT.Copy).then_inc(mix_hi_made, 1)

                def pool_hi(i):
                    act.wait_ge(pool_done, i + 1)
                    if i >= 2:
                        act.wait_ge(pm_made, i - 1)
                    act.activation(act_hi[:, PO + i % 2], pool_sums[i % 2][(HEADS - i) % 2], ACT.Copy).then_inc(pool_hi_made, 1)

                def pool_mixed_hi(i):
                    g = HEADS - 1 - i
                    act.wait_ge(pm_made, i + 1)
                    act.activation(act_hi[:, QK + HEADS + g], ps[:, 2 + i % 2], ACT.Copy,
                                   scale=scalar_of(V_PSC + g)).then_inc(pmx_hi, 1)

                weights_of(0)
                for tb in range(TB):
                    act.wait_ge(unit_used, V_UNIT[3] + 1)
                    act.activation(act_hi[:, VB + tb], ps[:, v_bank[tb]], ACT.Copy, scale=rcol[:, tb:tb + 1]
                                   ).then_inc(v_hi_made, 1)
                probs_hi(0)
                act.wait_ge(qk_made, 2 * HEADS)
                copy_r(1)
                split_next()
                split_next()
                act.wait_ge(pw_in, 16)
                act.activation(act_hi[:, PW], arena[:, 4], ACT.Copy).then_inc(pw_hi_made, 1)
                weights_of(1)
                for h in range(HEADS):
                    if h:
                        if h + 1 < HEADS:
                            copy_r(h + 1)
                        probs_hi(h)
                        if h == 1:
                            split_next()
                    else:
                        square_num(0)
                    if 1 <= h < HEADS - 1:
                        weights_of(h + 1)
                    gate(h)
                    if h:
                        split_next()
                        mixed_hi(h - 1)
                        square_num(h)
                split_next()
                mixed_hi(HEADS - 1)
                split_next()
                pool_hi(0)
                split_next()
                pool_hi(1)
                pool_mixed_hi(0)
                pool_hi(2)
                split_next()
                pool_mixed_hi(1)
                pool_hi(3)
                pool_mixed_hi(2)
                pool_mixed_hi(3)
                assert nxt[0] == WO_UNIT + SLOTS

            for i in range(KD):
                n, part = first_part(i)
                act.wait_ge(first_in[i] if i < KD - 2 else raw_in[n], 16)
                act.activation(w_hi[:, n, part], raw[:, n, part], ACT.Copy).then_inc(first_hi if i < KD - 2 else hi_made, 1)
                if i == 0:
                    act.wait_ge(vec_in, 16)
                prep_x(i, 0)
            square_x(POOL_SQ, 0)
            square_x(POOL_SQ + 1, 0)
            act.wait_ge(early_in, 16)
            split_hi(2, 2, 2, True)
            for d in range(POOL_SQ + 2, KD):
                square_x(d, 0)
            split_hi(3, 3, 2, True)
            ffn_up(UP1, 0)
            out_blocks(DN1, DN_UNITS, 1)
            mixer()
            out_blocks(WO_UNIT, 1, 2)
            ffn_up(UP2, 1)
            out_blocks(DN2, DN_UNITS, 3)

        @block.gpsimd
        def _(pool):
            for i, t in enumerate((ident, ones, mask)):
                pool.dma_start(t[:], consts[i]).then_inc(const_in, 16)
            pool.dma_start(arena[:, 4], pool_w).then_inc(pw_in, 16)
            for d in range(POOL_SQ):
                pool.wait_ge(x_in[d], 16)
                if d == 0:
                    pool.tensor_tensor(ssq, x[:, d], x[:, d], ALU.mult).then_inc(ssq_made, 1)
                    continue
                pool.tensor_tensor(sq[d % 2], x[:, d], x[:, d], ALU.mult).then_inc(pool_sq, 1)
                pool.wait_ge(pool_sq, d)
                pool.wait_ge(ssq_made, d)
                pool.tensor_tensor(ssq, ssq, sq[d % 2], ALU.add).then_inc(ssq_made, 1)
            pool.wait_ge(const_in, 16 * 3)
            for h in range(HEADS):
                pool.wait_ge(r_copied, h + 1)
                if h == 0:
                    pool.wait_ge(cols_made, 1)
                else:
                    pool.wait_ge(e_made, h)
                for S in range(TB):
                    at = slice(S * P, (S + 1) * P)
                    ins = pool.tensor_tensor(r_diag[:, at], r_all[h % 2][:, at], mask[:], ALU.add)
                ins.then_inc(r_diag_made, 1)

                pool.wait_ge(p_made, h + 1)
                if h >= 1:
                    pool.wait_ge(num_made, h)
                pool.tensor_copy(key_sum[:, 0:P], probs[:, 0:P])
                pool.tensor_tensor(key_sum[:, P:T], probs[:, P:T], probs[:, S_OFF[1]:S_OFF[1] + 3 * P],
                                   ALU.add).then_inc(ks_step, 1)
                for S in (2, 3):
                    pool.wait_ge(ks_step, (TB - 2) * h + S - 1)
                    add = pool.tensor_tensor(key_sum[:, S * P:T], key_sum[:, S * P:T],
                                             probs[:, S_OFF[S]:S_OFF[S] + T - S * P], ALU.add)
                    add.then_inc(ks_step if S == 2 else ks_made, 1)

            win = 0
            for i in range(HEADS):
                g = HEADS - 1 - i
                pool.wait_ge(pu_made, i + 1)
                src = pool_u[i % 2]
                for s in range(g + 1):
                    dst = pool_sums[i % 2][s % 2]
                    sh = 1 << s
                    if s > 0:
                        pool.wait_ge(win_step, win)
                    pool.tensor_copy(dst[:, 0:sh], src[:, 0:sh])
                    pool.tensor_tensor(dst[:, sh:T], src[:, sh:T], src[:, 0:T - sh], ALU.add).then_inc(win_step, 1)
                    win += 1
                    src = dst

            pool.wait_ge(last_rinv, 1)
            for d in range(KD):
                pool.wait_ge(gained, d + 1)
                pool.tensor_tensor(x[:, d, 0:HALF], x[:, d, 0:HALF], rinv[:, 0:HALF], ALU.mult).then_inc(ya_made, 1)

        @block.vector
        def _(dve):
            def split_lo(k, seen):
                dve.wait_ge(hi_made, seen + 1)
                dve.tensor_tensor(w_lo[:, k % SLOTS], raw[:, k % RAWS], f32(w_hi[:, k % SLOTS]),
                                  ALU.subtract).then_inc(lo_made, 1)

            def split_xg(d, stage):
                dve.wait_ge(xhi_made, KD * stage + d + 1)
                dve.scalar_tensor_tensor(xg_lo[:, d], x[:, d], scalar_of(V_GAIN + stage * KD + d),
                                         f32(xg_hi[:, d]), ALU.mult, ALU.subtract).then_inc(xg_made, 1)

            def add_square(d, stage):
                n = KD * stage + d
                dve.wait_ge(sq_made, n - POOL_SQ + 1)
                if d == 0:
                    dve.wait_ge(ssq_zero, stage)
                else:
                    dve.wait_ge(ssq_made, n)
                dve.tensor_tensor(ssq, ssq, sq[n % 2], ALU.add).then_inc(ssq_made, 1)

            def clear_squares(stage):
                dve.wait_ge(ms_made, stage)
                dve.memset(ssq, 0.0).then_inc(ssq_zero, 1)

            def rsqrt(step, count):
                def then(ins):
                    nonlocal count
                    ins.then_inc(step, 1)
                    count += 1
                    dve.wait_ge(step, count)

                then(dve.tensor_scalar(ycol[:].bitcast(I32), acol[:].bitcast(I32), 1, None, ALU.logical_shift_right))
                then(dve.tensor_scalar(ycol[:].bitcast(I32), ycol[:].bitcast(I32), -1.0, RSQRT_SEED, ALU.mult, ALU.add))
                for _ in range(3):
                    then(dve.scalar_tensor_tensor(tcol[:], ycol[:], -0.5, acol[:], ALU.mult, ALU.mult))
                    then(dve.tensor_tensor(tcol[:], tcol[:], ycol[:], ALU.mult))
                    then(dve.scalar_tensor_tensor(ycol[:], tcol[:], 1.5, ycol[:], ALU.add, ALU.mult))
                return count

            def inverse_rms(stage):
                base = STEPS * stage
                dve.wait_ge(ms_made, stage + 1)
                dve.tensor_scalar(acol[:], ps_rep[:, 0:TB], EPS, None, ALU.add).then_inc(col_step, 1)
                dve.wait_ge(col_step, base + 1)
                done = rsqrt(col_step, base + 1)
                assert done == base + STEPS
                if stage == 1:
                    dve.tensor_copy(rcol[:], ycol[:])

            def take_rinv(stage):
                dve.wait_ge(rep_made, stage + 1)
                dve.tensor_copy(rinv[:], ps_rep).then_inc(rinv_made, 1)
                dve.wait_ge(rinv_made, stage + 1)

            def ffn_up(base, p, stage):
                def step(f, j, first=False):
                    n = base + 2 * j
                    g, u = gs[j % 2], us[j % 2]
                    G, U = ps[:, 2 * (j % 2)], ps[:, 2 * (j % 2) + 1]
                    dve.wait_ge(unit_used, f * 2 + (base + 2))
                    dve.tensor_tensor(g, G, rinv[:], ALU.mult).then_inc(gate_scaled, 1)
                    dve.tensor_tensor(u, U, rinv[:], ALU.mult).then_inc(up_scaled, 1)
                    if not first:
                        split_lo(n + SLOTS, f * 2 + (base + SLOTS))
                    dve.wait_ge(silu_made, f + (p * FB + 1))
                    dve.wait_ge(up_scaled, f + (p * FB + 1))
                    dve.tensor_tensor(u, u, g, ALU.mult).then_inc(prod_made, 1)
                    split_lo(n + SLOTS + 1, f * 2 + (base + SLOTS + 1))
                    hi = act_hi[:, bass.ds(f, 1)].rearrange("p a n -> p (a n)")
                    lo = act_lo[:, bass.ds(f, 1)].rearrange("p a n -> p (a n)")
                    dve.wait_ge(prod_made, f + (p * FB + 1))
                    dve.tensor_scalar(hi, u, 1.0, None, ALU.mult).then_inc(act_hi_made, 1)
                    dve.wait_ge(act_hi_made, f + (p * FB + 1))
                    dve.tensor_tensor(lo, u, f32(hi), ALU.subtract).then_inc(act_made, 1)

                inverse_rms(stage)
                clear_squares(stage + 1)
                split_lo(base + SLOTS, base + SLOTS)
                take_rinv(stage)
                step(0, 0, True)
                step(1, 1)
                with dve.Fori(1, FB // 2) as it:
                    step(it * 2, 2)
                    step(it * 2 + 1, 3)

            def out_blocks(base, per, stage, factor, banks):
                for d in range(KD if stage < 3 else KD - 1):
                    n = base + per * d
                    for i in range(per - 1):
                        if n + SLOTS + i < N_UNITS:
                            split_lo(n + SLOTS + i, n + SLOTS + i)
                    dve.wait_ge(unit_used, n + per)
                    dve.scalar_tensor_tensor(x[:, d], ps[:, 4 + d % banks], factor, x[:, d],
                                             ALU.mult, ALU.add).then_inc(x_new, 1)
                    if n + SLOTS + per - 1 < N_UNITS:
                        split_lo(n + SLOTS + per - 1, n + SLOTS + per - 1)
                    if stage < 3:
                        dve.wait_ge(x_new, KD * (stage - 1) + d + 1)
                        split_xg(d, stage)
                    add_square(d, stage)

            def mixer():
                nxt = [MIX + SLOTS]

                def split_next():
                    split_lo(nxt[0], nxt[0])
                    nxt[0] += 1

                inverse_rms(1)
                take_rinv(1)
                R = slice(0, HEADS)
                fr = slice(32, 32 + HEADS)
                gsc, lf = arena[:, 0], arena[:, 2]

                def gates_in():
                    dve.tensor_tensor(arena[0:36, 0], ps[0:36, 2], rinv[0:36, :], ALU.mult).then_inc(g_dve, 1)
                    dve.wait_ge(g_dve, 1)
                    dve.tensor_scalar(lf[fr], gsc[fr], vec[fr, V_BG:V_BG + 1], 0.0, ALU.add, ALU.min).then_inc(g_dve, 1)
                    dve.tensor_scalar(gsc[R], gsc[R], vec[R, V_BG:V_BG + 1], None, ALU.add).then_inc(g_dve, 1)

                B, M, m = arena[R, 1], arena[R, 5], arena[R, 3]

                def gates_then(ins, count):
                    ins.then_inc(g_dve, 1)
                    dve.wait_ge(g_dve, count)

                def gates_first():
                    dve.wait_ge(g_dve, 3)
                    dve.wait_ge(g_act, 3)
                    gates_then(dve.tensor_tensor(lf[fr], lf[fr], arena[fr, 1], ALU.subtract), 4)
                    gates_then(dve.tensor_copy(lf[R], lf[fr]), 5)
                    gates_then(dve.tensor_tensor_scan(B, lf[R], lf[R], 0.0, ALU.add, ALU.min), 6)
                    gates_then(dve.tensor_tensor(B, gsc[R], B, ALU.subtract), 7)

                def gates_second():
                    gates_then(dve.tensor_tensor_scan(M, B, B, 0.0, ALU.max, ALU.max), 8)
                    gates_then(dve.tensor_scalar(neg_m[0], M, -1.0, None, ALU.mult), 9)
                    dve.scalar_tensor_tensor(neg_m[1], M, -1.0, f32(neg_m[0]), ALU.mult, ALU.subtract)
                    for h in range(HEADS):
                        dve.tensor_scalar(sel[:, h * P:(h + 1) * P], ones[R, :], ident[R, h:h + 1], None, ALU.mult)
                    dve.tensor_tensor_scan(m, lf[R], gsc[R], 0.0, ALU.add, ALU.max).then_inc(cm_made, 1)

                def taps(i):
                    b = i // 2 + HEADS * (i % 2)
                    u, a = work[:, i % 2], work[:, 2 + i % 2]
                    dve.wait_ge(u_made, i + 1)
                    dve.wait_ge(conv0, i + 1)
                    for back in range(1, 4):
                        ins = dve.scalar_tensor_tensor(a[:, back:T], u[:, 0:T - back],
                                                       scalar_of(V_CONVW + 4 * b + 3 - back), a[:, back:T],
                                                       ALU.mult, ALU.add)
                        if back < 3:
                            ins.then_inc(conv_step, 1)
                            dve.wait_ge(conv_step, 2 * i + back)
                    ins.then_inc(conv_done, 1)

                def qk_lo(i):
                    b = i // 2 + HEADS * (i % 2)
                    dve.wait_ge(qk_hi_made, i + 1)
                    dve.scalar_tensor_tensor(act_lo[:, QK + b], work[:, 2 + i % 2], K_SCALE if i % 2 else 1.0,
                                             f32(act_hi[:, QK + b]), ALU.mult, ALU.subtract).then_inc(qk_made, 1)

                gates_in()
                split_next()
                pending = None
                for n in range(MIX + 1, V_UNIT[2]):
                    if n in QK_UNIT:
                        i = QK_UNIT.index(n)
                        dve.wait_ge(unit_used, n + 1)
                        dve.tensor_tensor(work[:, i % 2], ps[:, qk_bank[i % 3]], rinv[:], ALU.mult).then_inc(u_made, 1)
                    if pending is not None:
                        taps(pending)
                    if n < QK_UNIT[7]:
                        split_next()
                        if pending is not None:
                            qk_lo(pending)
                    pending = i if n in QK_UNIT else None
                    if n == V_UNIT[0]:
                        gates_first()
                    if n == V_UNIT[1]:
                        gates_second()
                dve.wait_ge(cols_made, 1)
                dve.tensor_copy(cols[:], ps[:, 3, 0:2 * TB * HEADS]).then_inc(cols_made, 1)
                taps(7)
                qk_lo(6)
                split_next()
                qk_lo(7)
                dve.wait_ge(cols_made, 3)
                dve.scalar_tensor_tensor(em2[:], emcol[:], EPS, emcol[:], ALU.mult, ALU.mult).then_inc(cols_made, 1)

                def gate(h):
                    dve.wait_ge(unit_used, O_UNIT + h + 1)
                    dve.tensor_tensor(gate_of[h % 2], ps[:, proj_bank(h)], rinv[:], ALU.mult).then_inc(o_scaled, 1)

                def probs_of(h):
                    dve.wait_ge(sc_made, h + 1)
                    dve.wait_ge(e_made, h + 1)
                    dve.tensor_tensor(probs, probs, ps_sc, ALU.mult).then_inc(p_made, 1)

                def probs_lo(h):
                    dve.wait_ge(p_made, h + 1)
                    dve.wait_ge(p_hi_made, h + 1)
                    dve.tensor_tensor(p_lo, probs, f32(p_hi), ALU.subtract).then_inc(p_split, 1)

                def head_columns(h):
                    dve.wait_ge(num_made, h + 1)
                    count = HSTEPS * h

                    def then(ins):
                        nonlocal count
                        ins.then_inc(hcol_step, 1)
                        count += 1
                        dve.wait_ge(hcol_step, count)

                    then(dve.tensor_copy(qcol[:], ps_col[:, 0:SUMW * TB:SUMW]))
                    then(dve.scalar_tensor_tensor(dcol[:], qcol[:], EPS, qcol[:], ALU.mult, ALU.mult))
                    if h == 0:
                        dve.wait_ge(cols_made, 4)
                    then(dve.tensor_tensor(dcol[:], dcol[:], em2[:, h:16:4], ALU.max))

                def head_product(h):
                    dve.wait_ge(sqn_made, h + 1)
                    dve.wait_ge(o_made, h + 1)
                    if h >= 1:
                        dve.wait_ge(mix_made, h)
                    dve.scalar_tensor_tensor(t1, ps_num, scalar_of(V_MH + h), gate_of[h % 2],
                                             ALU.mult, ALU.mult).then_inc(t1_made, 1)

                def head_rsqrt(h):
                    count = HSTEPS * h + 3
                    dve.wait_ge(ms_h, h + 1)
                    dve.scalar_tensor_tensor(acol[:], ps_col[:, SUMW * TB:SUMW * TB + TB], TINY, dcol[:],
                                             ALU.add, ALU.add).then_inc(hcol_step, 1)
                    dve.wait_ge(hcol_step, count + 1)
                    rsqrt(hcol_step, count + 1)

                def mixed(h):
                    dve.wait_ge(h_rep, h + 1)
                    dve.tensor_tensor(t1, t1, ps_rep, ALU.mult).then_inc(hm_made, 1)

                def mixed_lo(h):
                    dve.wait_ge(hm_made, h + 1)
                    dve.wait_ge(mix_hi_made, h + 1)
                    dve.tensor_tensor(act_lo[:, QK + h], t1, f32(act_hi[:, QK + h]),
                                      ALU.subtract).then_inc(mix_made, 1)

                def pool_in(i):
                    dve.wait_ge(unit_used, PL_UNIT + i + 1)
                    dve.tensor_tensor(pool_u[i % 2], ps[:, proj_bank(HEADS + i)], rinv[:], ALU.mult).then_inc(pu_made, 1)

                def pool_mean(i):
                    g = HEADS - 1 - i
                    u, s, dst = pool_u[i % 2], pool_sums[i % 2][g % 2], pool_sums[i % 2][(g + 1) % 2]
                    dve.wait_ge(win_step, sum(HEADS - k for k in range(i + 1)))
                    dve.wait_ge(pu_made, i + 1)
                    inv = vec[:, V_INV + MAXWIN * g:V_INV + MAXWIN * (g + 1)]
                    dve.tensor_tensor(dst[:, 0:MAXWIN], s[:, 0:MAXWIN], inv, ALU.mult).then_inc(pool_step, 1)
                    dve.scalar_tensor_tensor(dst[:, MAXWIN:T], s[:, MAXWIN:T], 1.0 / WINDOWS[g], u[:, MAXWIN:T],
                                             ALU.mult, ALU.subtract)
                    dve.wait_ge(pool_step, i + 1)
                    dve.tensor_tensor(dst[:, 0:MAXWIN], dst[:, 0:MAXWIN], u[:, 0:MAXWIN],
                                      ALU.subtract).then_inc(pool_done, 1)

                def pool_lo(i):
                    dve.wait_ge(pool_done, i + 1)
                    dve.wait_ge(pool_hi_made, i + 1)
                    dve.tensor_tensor(act_lo[:, PO + i % 2], pool_sums[i % 2][(HEADS - i) % 2],
                                      f32(act_hi[:, PO + i % 2]), ALU.subtract).then_inc(pool_made, 1)

                def pool_mixed_lo(i):
                    g = HEADS - 1 - i
                    dve.wait_ge(pmx_hi, i + 1)
                    dve.scalar_tensor_tensor(act_lo[:, QK + HEADS + g], ps[:, 2 + i % 2], scalar_of(V_PSC + g),
                                             f32(act_hi[:, QK + HEADS + g]), ALU.mult, ALU.subtract
                                             ).then_inc(pmx_made, 1)

                probs_of(0)
                for tb in range(TB):
                    dve.wait_ge(v_hi_made, tb + 1)
                    dve.scalar_tensor_tensor(act_lo[:, VB + tb], ps[:, v_bank[tb]], rcol[:, tb:tb + 1],
                                             f32(act_hi[:, VB + tb]), ALU.mult, ALU.subtract).then_inc(v_made, 1)
                probs_lo(0)
                split_next()
                split_next()
                dve.wait_ge(pw_hi_made, 1)
                dve.tensor_tensor(act_lo[:, PW], arena[:, 4], f32(act_hi[:, PW]), ALU.subtract).then_inc(pw_made, 1)
                for h in range(HEADS):
                    if h:
                        head_product(h - 1)
                        if h % 2 == 1:
                            head_rsqrt(h - 1)
                            probs_lo(h)
                        else:
                            probs_lo(h)
                            head_rsqrt(h - 1)
                    if h == 1:
                        split_next()
                    gate(h)
                    if h == 0:
                        head_columns(0)
                    if h == 1:
                        mixed(0)
                    if h + 1 < HEADS:
                        probs_of(h + 1)
                    if h == 1:
                        head_columns(1)
                    if h >= 2:
                        mixed(h - 1)
                    if h:
                        split_next()
                        mixed_lo(h - 1)
                    if h >= 2:
                        head_columns(h)
                head_product(HEADS - 1)
                head_rsqrt(HEADS - 1)
                pool_in(0)
                split_next()
                mixed(HEADS - 1)
                mixed_lo(HEADS - 1)
                pool_in(1)
                split_next()
                pool_mean(0)
                pool_lo(0)
                pool_in(2)
                split_next()
                pool_mean(1)
                pool_lo(1)
                pool_mixed_lo(0)
                pool_mean(2)
                pool_lo(2)
                pool_in(3)
                split_next()
                pool_mixed_lo(1)
                pool_mean(3)
                pool_lo(3)
                pool_mixed_lo(2)
                pool_mixed_lo(3)
                clear_squares(2)
                assert nxt[0] == WO_UNIT + SLOTS

            def last_block():
                d = KD - 1
                for a in range(2):
                    at = slice(a * HALF, (a + 1) * HALF)
                    dve.wait_ge(last_made, a + 1)
                    dve.scalar_tensor_tensor(x[:, d, at], ps[:, 5 - 2 * a, 0:HALF], 0.5, x[:, d, at],
                                             ALU.mult, ALU.add).then_inc(last_x, 1)
                    dve.wait_ge(last_x, a + 1)
                    if a == 0:
                        dve.wait_ge(ssq_made, 4 * KD - 2)
                    dve.tensor_tensor(sq[1][:, at], x[:, d, at], x[:, d, at], ALU.mult).then_inc(last_sq, 1)
                    inverse_rms(3 + a)
                    dve.wait_ge(rep_made, 4 + a)
                    if a == 0:
                        dve.tensor_copy(rinv[:, at], ps[:, 6, at]).then_inc(last_rinv, 1)
                for d in range(KD):
                    dve.wait_ge(gained, d + 1 if d < KD - 1 else KD + 1)
                    dve.tensor_tensor(x[:, d, at], x[:, d, at], ps[:, 6, at], ALU.mult).then_inc(y_made, 1)

            dve.memset(zeros, 0.0).then_inc(zeros_made, 1)
            for i in range(KD):
                n, part = first_part(i)
                dve.wait_ge(*((first_hi, i + 1) if i < KD - 2 else (hi_made, n + 1)))
                dve.tensor_tensor(w_lo[:, n, part], raw[:, n, part], f32(w_hi[:, n, part]),
                                  ALU.subtract).then_inc(first_lo if i < KD - 2 else lo_made, 1)
                if i == 0:
                    dve.wait_ge(vec_in, 16)
                split_xg(i, 0)
            dve.wait_ge(const_in, 16 * 3)
            add_square(POOL_SQ, 0)
            add_square(POOL_SQ + 1, 0)
            split_lo(2, 2)
            for d in range(POOL_SQ + 2, KD):
                add_square(d, 0)
            split_lo(3, 3)
            ffn_up(UP1, 0, 0)
            out_blocks(DN1, DN_UNITS, 1, 0.5, 2)
            mixer()
            out_blocks(WO_UNIT, 1, 2, 1.0, 4)
            ffn_up(UP2, 1, 2)
            out_blocks(DN2, DN_UNITS, 3, 0.5, 2)
            last_block()


def _blocks(w):
    rows, cols = w.shape
    return w.reshape(rows // P, P, cols // P, P).transpose(2, 1, 0, 3).reshape(cols // P, P, rows)


def kernel(**inputs):
    import concourse.bacc as bacc
    from concourse.bass_utils import run_bass_kernel_spmd

    a = {k: np.asarray(v) for k, v in inputs.items()}

    def ffn(p):
        gate, up = _blocks(a[p + "_w_gate"][0]), _blocks(a[p + "_w_up"][0])
        yield np.stack([gate, up], 1).reshape(2 * FB, P, UNIT)
        down = np.zeros((KD, P, DN_UNITS, UNIT), np.float32)
        down.reshape(KD, P, DN_UNITS * UNIT)[:, :, :FF] = _blocks(a[p + "_w_down"][0])
        yield down.transpose(0, 2, 1, 3).reshape(DN_UNITS * KD, P, UNIT)

    def mixer():
        w = a["w_in"][0]
        half = D // 2
        gates = np.zeros((D, P), np.float32)
        gates[:, 0:HEADS] = w[:, 4 * half:4 * half + HEADS]
        gates[:, 32:32 + HEADS] = w[:, 4 * half + HEADS:4 * half + 2 * HEADS]
        yield _blocks(gates)
        q, k = _blocks(w[:, 0:half]), _blocks(w[:, half:2 * half])
        qk = np.stack([q, k], 1).reshape(2 * HEADS, P, UNIT)
        v = w[:, 2 * half:3 * half].reshape(4, 2, P, half).transpose(0, 2, 1, 3).reshape(4, P, UNIT)
        place = {n: qk[i] for i, n in enumerate(QK_UNIT)} | {n: v[i] for i, n in enumerate(V_UNIT)}
        yield np.stack([place[n] for n in sorted(place)])
        yield _blocks(w[:, 3 * half:4 * half])
        yield _blocks(w[:, 4 * half + 2 * HEADS:])[::-1]
        yield _blocks(a["w_out"][0])

    weights = np.concatenate([*ffn("ffn1"), *mixer(), *ffn("ffn2")])
    pool_w = a["pool_w"][0].transpose(1, 0, 2).reshape(P, HEADS * P)

    vecs = np.zeros((P, N_VEC), np.float32)

    def columns(at, v):
        vecs[:, at:at + v.size // P] = v.reshape(-1, P).T

    for i, g in enumerate((a["ffn1_norm"][0], a["mix_norm"][0], a["ffn2_norm"][0], a["final_norm"])):
        columns(V_GAIN + KD * i, g)
    vecs[:, V_CONVW:V_CONVB] = a["conv_w"][0].reshape(4, KD, P).transpose(2, 1, 0).reshape(P, 4 * KD)
    columns(V_CONVB, a["conv_b"][0])
    columns(V_MH, a["mh_norm"][0])
    columns(V_PSC, a["pool_scale"][0])
    vecs[0:HEADS, V_BG] = a["b_gates"][0, 0:HEADS]
    vecs[32:32 + HEADS, V_BG] = a["b_gates"][0, HEADS:]
    vecs[:, V_MEAN_D], vecs[:, V_MEAN_H] = 1.0 / D, 1.0 / P
    for g, win in enumerate(WINDOWS):
        at = V_INV + MAXWIN * g
        vecs[:, at:at + MAXWIN] = (1.0 / np.minimum(np.arange(1, MAXWIN + 1), win)).astype(np.float32)
    causal = np.arange(P)[:, None] <= np.arange(P)[None, :]
    consts = np.stack([np.eye(P), np.ones((P, P)), np.where(causal, 0.0, -1e30)]).astype(np.float32)

    arrays = {"weights": weights, "pool_w": pool_w, "x_t": a["x"][0].T, "vecs": vecs, "consts": consts}
    arrays = {k: np.ascontiguousarray(v) for k, v in arrays.items()}
    nc = bacc.Bacc("TRN2", target_bir_lowering=False, num_devices=1)
    args = [nc.dram_tensor(k, v.shape, F32, kind="ExternalInput").ap() for k, v in arrays.items()]
    out = nc.dram_tensor("out", (D, T), F32, kind="ExternalOutput").ap()
    build_layer(nc, *args, out)
    r = run_bass_kernel_spmd(nc, [arrays], core_ids=[0])
    return np.ascontiguousarray(r.results[0]["out"].T).reshape(1, T, D)
```
